# Optimizing a Trainium2 kernel written in Bass

```python
import jax
import jax.numpy as jnp
from jax import lax
import numpy as np

D_MODEL = 1024
BATCH = 1
SEQ = 512
DEPTH = 2

GLA_HEADS = 4
GLA_DK = 64
GLA_DV = 128
GLA_GATE_RANK = 16
GLA_TAU = 16.0
GLA_CHUNK = 64
MLSTM_HEADS = 4
MLSTM_DH = 128
MLSTM_CONV = 4
MLSTM_CHUNK = 64
SB_HEADS = 8
SB_DH = 64
SB_BLOCK = 128
DIL_PAIRS = ((128, 1), (512, 4), (2048, 16))
DIL_HEADS_PER_GROUP = 4
DIL_DH = 64
DIL_HEADS = len(DIL_PAIRS) * DIL_HEADS_PER_GROUP
N_REL_BUCKETS = 32
REL_MAX_DIST = 2048
D_FF = ((8 * D_MODEL + 3 * 256 - 1) // (3 * 256)) * 256
LN_EPS = 1e-5
RES_ALPHA = (2 * DEPTH) ** 0.25
OUT_BETA = (8 * DEPTH) ** -0.25
ADA_SCALE = 0.1
NEG_INF = -1e30
N_EVEN = (DEPTH + 1) // 2
N_ODD = DEPTH // 2

GLA_QK = GLA_HEADS * GLA_DK
GLA_V = GLA_HEADS * GLA_DV
ML_W = MLSTM_HEADS * MLSTM_DH
AB_SPLITS = (GLA_QK, GLA_QK, GLA_V, GLA_V, GLA_GATE_RANK, 2 * ML_W, ML_W, MLSTM_HEADS, MLSTM_HEADS, ML_W)
AB_IN = sum(AB_SPLITS)
AB_OUT = GLA_V + ML_W
SB_W = SB_HEADS * SB_DH
DIL_W = DIL_HEADS * DIL_DH
CD_SPLITS = (SB_W, SB_W, SB_W, DIL_W, DIL_W, DIL_W)
CD_IN = sum(CD_SPLITS)
CD_OUT = SB_W + DIL_HEADS_PER_GROUP * DIL_DH

kernel_name = 'hybrid_gla_mlstm_stickbreak_dilated'

def split_cols(t, sizes):
    idx = [int(s) for s in np.cumsum(sizes)[:-1]]
    return jnp.split(t, idx, axis=-1)

def layer_norm(x, g, b):
    xf = x.astype(jnp.float32)
    mu = jnp.mean(xf, -1, keepdims=True)
    var = jnp.mean(jnp.square(xf - mu), -1, keepdims=True)
    y = (xf - mu) * lax.rsqrt(var + LN_EPS)
    return (y * g.astype(jnp.float32) + b.astype(jnp.float32)).astype(x.dtype)

def head_norm(x, g):
    mu = jnp.mean(x, -1, keepdims=True)
    var = jnp.mean(jnp.square(x - mu), -1, keepdims=True)
    return (x - mu) * lax.rsqrt(var + LN_EPS) * g.astype(jnp.float32).reshape(x.shape[-2], x.shape[-1])

def causal_dwconv(x, w, b):
    k_w, ch = w.shape
    y = lax.conv_general_dilated(x, w.astype(x.dtype)[:, None, :], window_strides=(1,),
                                 padding=((k_w - 1, 0),), dimension_numbers=('NWC', 'WIO', 'NWC'),
                                 feature_group_count=ch)
    return y + b.astype(x.dtype)

def gla_chunked(q, k, v, log_a):
    bsz, s_len, h, dk = q.shape
    dv = v.shape[-1]
    cl = GLA_CHUNK
    nc = s_len // cl
    q, k, v, log_a = [t.reshape(bsz, nc, cl, h, t.shape[-1]) for t in (q, k, v, log_a)]
    b = jnp.cumsum(log_a, axis=2)
    b_last = b[:, :, -1]
    q_in = q * jnp.exp(b)
    k_in = k * jnp.exp(-b)
    tril = np.tril(np.ones((cl, cl), dtype=bool))
    scores = jnp.where(tril, jnp.einsum('bnihk,bnjhk->bnhij', q_in, k_in), 0.0)
    o_intra = jnp.einsum('bnhij,bnjhv->bnihv', scores, v)
    kv_chunk = jnp.einsum('bnjhk,bnjhv->bnhkv', k * jnp.exp(b_last[:, :, None] - b), v)
    decay = jnp.exp(b_last)

    def step(state, inp):
        dec, kv = inp
        return dec[..., None] * state + kv, state

    init = jnp.zeros((bsz, h, dk, dv), jnp.float32)
    _, s_before = lax.scan(step, init, (jnp.moveaxis(decay, 1, 0), jnp.moveaxis(kv_chunk, 1, 0)))
    o_inter = jnp.einsum('bnihk,nbhkv->bnihv', q_in, s_before)
    return (o_intra + o_inter).reshape(bsz, s_len, h, dv)

def mlstm_chunked(q, k, v, i_pre, log_f):
    bsz, s_len, h, d = q.shape
    cl = MLSTM_CHUNK
    nc = s_len // cl
    q, k, v = [t.reshape(bsz, nc, cl, h, d) for t in (q, k, v)]
    i_pre, log_f = [t.reshape(bsz, nc, cl, h) for t in (i_pre, log_f)]
    b = jnp.cumsum(log_f, axis=2)
    b_last = b[:, :, -1]
    tril = np.tril(np.ones((cl, cl), dtype=bool))[:, :, None]
    d_log = jnp.where(tril, b[:, :, :, None, :] - b[:, :, None, :, :] + i_pre[:, :, None, :, :], NEG_INF)
    w_end = b_last[:, :, None, :] - b + i_pre

    def step(carry, inp):
        c_bar, n_bar, m = carry
        k_c, v_c, w_c, bl = inp
        m_new = jnp.maximum(bl + m, jnp.max(w_c, axis=1))
        sc = jnp.exp(bl + m - m_new)
        wj = jnp.exp(w_c - m_new[:, None, :])
        c_new = sc[..., None, None] * c_bar + jnp.einsum('bjh,bjhv,bjhk->bhvk', wj, v_c, k_c)
        n_new = sc[..., None] * n_bar + jnp.einsum('bjh,bjhk->bhk', wj, k_c)
        return (c_new, n_new, m_new), (c_bar, n_bar, m)

    init = (jnp.zeros((bsz, h, d, d), jnp.float32), jnp.zeros((bsz, h, d), jnp.float32),
            jnp.zeros((bsz, h), jnp.float32))
    xs = (jnp.moveaxis(k, 1, 0), jnp.moveaxis(v, 1, 0), jnp.moveaxis(w_end, 1, 0), jnp.moveaxis(b_last, 1, 0))
    _, (c_prev, n_prev, m_prev) = lax.scan(step, init, xs)
    inter_log = b + jnp.moveaxis(m_prev, 0, 1)[:, :, None, :]
    m_i = jnp.maximum(inter_log, jnp.max(d_log, axis=3))
    w_intra = jnp.exp(d_log - m_i[:, :, :, None, :])
    s_inter = jnp.exp(inter_log - m_i)
    a = w_intra * jnp.einsum('bnihd,bnjhd->bnijh', q, k)
    num = jnp.einsum('bnijh,bnjhd->bnihd', a, v) + s_inter[..., None] * jnp.einsum('bnihk,nbhvk->bnihv', q, c_prev)
    den = jnp.sum(a, axis=3) + s_inter * jnp.einsum('bnihk,nbhk->bnih', q, n_prev)
    hid = num / jnp.maximum(jnp.abs(den), jnp.exp(-m_i))[..., None]
    return hid.reshape(bsz, s_len, h, d)

def stick_breaking(q, k, v):
    bsz, s_len, h, dh = q.shape
    nq = s_len // SB_BLOCK
    scale = dh ** -0.5
    qb = q.reshape(bsz, nq, SB_BLOCK, h, dh).transpose(1, 0, 2, 3, 4)
    s_pos = jnp.arange(s_len)

    def block(args):
        q_blk, i = args
        z = jnp.einsum('bqhd,bkhd->bhqk', q_blk, k) * scale
        t_pos = i * SB_BLOCK + jnp.arange(SB_BLOCK)
        causal = s_pos[None, :] < t_pos[:, None]
        log_1m = jnp.where(causal, jax.nn.log_sigmoid(-z), 0.0)
        suffix = lax.cumsum(log_1m, axis=3, reverse=True)
        excl = jnp.pad(suffix[..., 1:], ((0, 0), (0, 0), (0, 0), (0, 1)))
        att = jnp.where(causal, jnp.exp(jax.nn.log_sigmoid(z) + excl), 0.0)
        return jnp.einsum('bhqk,bkhd->bqhd', att, v)

    out = lax.map(block, (qb, jnp.arange(nq)))
    return out.transpose(1, 0, 2, 3, 4).reshape(bsz, s_len, h, dh)

def t5_bucket(dist):
    max_exact = N_REL_BUCKETS // 2
    dd = np.maximum(dist, 1).astype(np.float64)
    large = max_exact + (np.log(dd / max_exact) / np.log(REL_MAX_DIST / max_exact)
                         * (N_REL_BUCKETS - max_exact)).astype(np.int32)
    large = np.minimum(large, N_REL_BUCKETS - 1)
    return np.where(dist < max_exact, dist, large).astype(np.int32)

def dilated_group(q, k, v, bias_tab, window, dil):
    bsz, s_len, h, dh = q.shape
    blk = window // dil
    unit = blk * dil
    sp = -(-s_len // unit) * unit
    n_sub = sp // dil
    nb = n_sub // blk

    def to_sub(t):
        t = jnp.pad(t, ((0, 0), (0, sp - s_len), (0, 0), (0, 0)))
        t = t.reshape(bsz, n_sub, dil, h, dh).transpose(0, 2, 1, 3, 4)
        return t.reshape(bsz, dil, nb, blk, h, dh)

    def with_prev(t):
        prev = jnp.pad(t[:, :, :-1], ((0, 0), (0, 0), (1, 0), (0, 0), (0, 0), (0, 0)))
        return jnp.concatenate([prev, t], axis=3)

    qs = to_sub(q)
    kk = with_prev(to_sub(k))
    vv = with_prev(to_sub(v))
    qi = np.arange(blk)[:, None]
    kj = np.arange(2 * blk)[None, :]
    delta = qi - kj + blk
    in_win = (delta >= 0) & (delta <= blk)
    valid = in_win[None] & ((np.arange(nb)[:, None, None] > 0) | (kj[None] >= blk))
    bucket = t5_bucket(np.clip(delta, 0, None) * dil)
    bias = jnp.transpose(bias_tab[bucket].astype(jnp.float32), (2, 0, 1))
    logits = jnp.einsum('brnqhd,brnkhd->brnhqk', qs, kk) * dh ** -0.5 + bias
    logits = jnp.where(valid[:, None], logits, NEG_INF)
    m = jnp.max(logits, axis=-1, keepdims=True)
    p = jnp.exp(logits - m)
    den = jnp.sum(p, axis=-1)
    o = jnp.einsum('brnhqk,brnkhd->brnqhd', p, vv) / jnp.swapaxes(den, -1, -2)[..., None]
    lse = jnp.swapaxes(m[..., 0] + jnp.log(den), -1, -2)

    def from_sub(t):
        rest = t.shape[4:]
        t = jnp.swapaxes(t.reshape((bsz, dil, n_sub) + rest), 1, 2)
        return t.reshape((bsz, sp) + rest)[:, :s_len]

    return from_sub(o), from_sub(lse)

def dilated_mixture(q, k, v, rel_bias):
    outs, lses = [], []
    for g, (window, dil) in enumerate(DIL_PAIRS):
        tab = rel_bias[:, g * DIL_HEADS_PER_GROUP:(g + 1) * DIL_HEADS_PER_GROUP]
        o, l = dilated_group(q[:, :, g], k[:, :, g], v[:, :, g], tab, window, dil)
        outs.append(o)
        lses.append(l)
    wts = jax.nn.softmax(jnp.stack(lses, 0), axis=0)
    return jnp.sum(wts[..., None] * jnp.stack(outs, 0), axis=0)

def gla_mlstm_mixer(h, w_in, wa_up, ba, gla_g, conv_w, conv_b, b_i, b_f, ml_g, w_out):
    bsz, s_len, _ = h.shape
    proj = (h @ w_in).astype(jnp.float32)
    qa, ka, va, ra, aa, qkb, vb, ib, fb, ob = split_cols(proj, AB_SPLITS)
    qa = qa.reshape(bsz, s_len, GLA_HEADS, GLA_DK) * GLA_DK ** -0.5
    ka = ka.reshape(bsz, s_len, GLA_HEADS, GLA_DK)
    va = va.reshape(bsz, s_len, GLA_HEADS, GLA_DV)
    log_a = jax.nn.log_sigmoid(aa @ wa_up.astype(jnp.float32) + ba.astype(jnp.float32)) / GLA_TAU
    oa = gla_chunked(qa, ka, va, log_a.reshape(bsz, s_len, GLA_HEADS, GLA_DK))
    oa = (head_norm(oa, gla_g).reshape(bsz, s_len, GLA_V)) * jax.nn.silu(ra)
    qkb = jax.nn.silu(causal_dwconv(qkb, conv_w, conv_b))
    qb_, kb_ = jnp.split(qkb, 2, axis=-1)
    qb_ = qb_.reshape(bsz, s_len, MLSTM_HEADS, MLSTM_DH)
    kb_ = kb_.reshape(bsz, s_len, MLSTM_HEADS, MLSTM_DH) * MLSTM_DH ** -0.5
    vb = vb.reshape(bsz, s_len, MLSTM_HEADS, MLSTM_DH)
    i_pre = ib + b_i.astype(jnp.float32)
    log_f = jax.nn.log_sigmoid(fb + b_f.astype(jnp.float32))
    hb = mlstm_chunked(qb_, kb_, vb, i_pre, log_f)
    hb = jax.nn.sigmoid(ob) * head_norm(hb, ml_g).reshape(bsz, s_len, ML_W)
    y = jnp.concatenate([oa, hb], axis=-1) @ w_out
    return y.astype(h.dtype)

def sb_dilated_mixer(h, w_in, rel_bias, w_out):
    bsz, s_len, _ = h.shape
    proj = (h @ w_in).astype(jnp.float32)
    qc, kc, vc, qd, kd, vd = split_cols(proj, CD_SPLITS)
    hc = lambda t: t.reshape(bsz, s_len, SB_HEADS, SB_DH)
    oc = stick_breaking(hc(qc), hc(kc), hc(vc)).reshape(bsz, s_len, SB_W)
    hd = lambda t: t.reshape(bsz, s_len, len(DIL_PAIRS), DIL_HEADS_PER_GROUP, DIL_DH)
    od = dilated_mixture(hd(qd), hd(kd), hd(vd), rel_bias).reshape(bsz, s_len, DIL_HEADS_PER_GROUP * DIL_DH)
    y = jnp.concatenate([oc, od], axis=-1) @ w_out
    return y.astype(h.dtype)

def swiglu(h, w1, w3, w2):
    return (jax.nn.silu(h @ w1) * (h @ w3)) @ w2

def setup_inputs(seed: int = 0) -> dict:
    key = jax.random.key(seed)
    ks = jax.random.split(key, 22)
    nrm = lambda k, shape, s: jax.random.normal(k, shape, jnp.float32) * s
    d = D_MODEL
    return {
        'x': nrm(ks[0], (BATCH, SEQ, d), 1.0),
        'c': nrm(ks[1], (BATCH, d), 1.0),
        'ada_w': nrm(ks[2], (DEPTH, d, 6 * d), ADA_SCALE * d ** -0.5),
        'ada_b': nrm(ks[3], (DEPTH, 6 * d), 0.01),
        'ln_g': 1.0 + nrm(ks[4], (DEPTH, 2, d), 0.02),
        'ln_b': nrm(ks[5], (DEPTH, 2, d), 0.02),
        'ab_w_in': nrm(ks[6], (N_EVEN, d, AB_IN), d ** -0.5),
        'gla_wa_up': nrm(ks[7], (N_EVEN, GLA_GATE_RANK, GLA_QK), GLA_GATE_RANK ** -0.5),
        'gla_ba': nrm(ks[8], (N_EVEN, GLA_QK), 0.1),
        'gla_norm_g': 1.0 + nrm(ks[9], (N_EVEN, GLA_V), 0.02),
        'ml_conv_w': nrm(ks[10], (N_EVEN, MLSTM_CONV, 2 * ML_W), MLSTM_CONV ** -0.5),
        'ml_conv_b': nrm(ks[11], (N_EVEN, 2 * ML_W), 0.01),
        'ml_b_i': nrm(ks[12], (N_EVEN, MLSTM_HEADS), 0.1),
        'ml_b_f': jnp.linspace(3.0, 6.0, MLSTM_HEADS)[None, :] + nrm(ks[13], (N_EVEN, MLSTM_HEADS), 0.1),
        'ml_norm_g': 1.0 + nrm(ks[14], (N_EVEN, ML_W), 0.02),
        'ab_w_out': nrm(ks[15], (N_EVEN, AB_OUT, d), OUT_BETA * AB_OUT ** -0.5),
        'cd_w_in': nrm(ks[16], (N_ODD, d, CD_IN), d ** -0.5),
        'rel_bias': nrm(ks[17], (N_REL_BUCKETS, DIL_HEADS), 0.5),
        'cd_w_out': nrm(ks[18], (N_ODD, CD_OUT, d), OUT_BETA * CD_OUT ** -0.5),
        'ffn_w1': nrm(ks[19], (DEPTH, d, D_FF), d ** -0.5),
        'ffn_w3': nrm(ks[20], (DEPTH, d, D_FF), d ** -0.5),
        'ffn_w2': nrm(ks[21], (DEPTH, D_FF, d), OUT_BETA * D_FF ** -0.5),
    }

def reference(x, c, ada_w, ada_b, ln_g, ln_b, ab_w_in, gla_wa_up, gla_ba, gla_norm_g, ml_conv_w, ml_conv_b,
              ml_b_i, ml_b_f, ml_norm_g, ab_w_out, cd_w_in, rel_bias, cd_w_out, ffn_w1, ffn_w3, ffn_w2):
    c_act = jax.nn.silu(c)
    for layer in range(DEPTH):
        mod = c_act @ ada_w[layer] + ada_b[layer]
        sh_m, sc_m, g_m, sh_f, sc_f, g_f = [t[:, None, :] for t in jnp.split(mod, 6, axis=-1)]
        hm = x * (1.0 + sc_m) + sh_m
        j = layer // 2
        if layer % 2 == 0:
            y = gla_mlstm_mixer(hm, ab_w_in[j], gla_wa_up[j], gla_ba[j], gla_norm_g[j], ml_conv_w[j], ml_conv_b[j],
                                ml_b_i[j], ml_b_f[j], ml_norm_g[j], ab_w_out[j])
        else:
            y = sb_dilated_mixer(hm, cd_w_in[j], rel_bias, cd_w_out[j])
        x = layer_norm(RES_ALPHA * x + (1.0 + g_m) * y, ln_g[layer, 0], ln_b[layer, 0])
        hf = x * (1.0 + sc_f) + sh_f
        yf = swiglu(hf, ffn_w1[layer], ffn_w3[layer], ffn_w2[layer])
        x = layer_norm(RES_ALPHA * x + (1.0 + g_f) * yf, ln_g[layer, 1], ln_b[layer, 1])
    return x


_drawn_inputs = setup_inputs


def setup_inputs(seed=0):
    import zlib

    import numpy as np

    out = dict(_drawn_inputs(seed))
    spreads = {}
    factors = {'ada_b': 4.543,
     'gla_wa_up': 3.403,
     'gla_ba': 8.0,
     'gla_norm_g': 141.75,
     'ml_conv_b': 8.0,
     'ml_b_i': 200.0,
     'ml_norm_g': 155.636,
     'rel_bias': 4.95}
    for name, (base, spread) in spreads.items():
        noise = np.random.default_rng([zlib.crc32(name.encode()), seed]).standard_normal(out[name].shape)
        drawn = base * np.exp(spread * noise) if base else spread * noise
        out[name] = jnp.asarray(drawn.astype(out[name].dtype))
    for name, factor in factors.items():
        out[name] = (out[name] * factor).astype(out[name].dtype)
    return out
```

```python
from contextlib import ExitStack

import numpy as np

import concourse.bass as bass
from concourse import mybir

ALU = mybir.AluOpType
ACT = mybir.ActivationFunctionType
F32 = mybir.dt.float32
F32R = mybir.dt.float32r
U32 = mybir.dt.uint32

P = 128
D = 1024
S = 512
KC = D // P
TB = S // P
D_FF = 2816
FC = D_FF // P
CHUNK = 64
NCH = S // CHUNK
ALPHA = 4 ** 0.25
EPS = 1e-5
TAU = 16.0
NEG = -1e30
SLOT = 1024
RAW = 4
RING = 4
DIL = ((128, 1), (512, 4), (2048, 16))
N_BUCKETS, REL_MAX = 32, 2048



def panel_slots(nk):
    return [(k, min(4, nk - k)) for k in range(0, nk, 4)]


def stage_table():
    table, n = {}, 0

    def add(name, count):
        nonlocal n
        table[name] = (n, count)
        n += count

    add("narrow", 1)
    for name in ("qa", "ka"):
        add(name, 2)
    add("va", 4)
    for p in range(4):
        add(f"qkb{p}", 2)
    for name in ("vb", "ra", "ob"):
        add(name, 4)
    for p in range(4):
        add(f"out0{p}", 2)
    for layer in (0, 1):
        if layer == 1:
            for name, panels in (("qc", 2), ("kc", 2), ("qd", 3), ("kd", 3)):
                for p in range(panels):
                    add(f"{name}{p}", 2)
            add("vc", 4)
            add("vd0", 4)
            add("vd1", 2)
            for p in range(4):
                add(f"out1{p}", 2)
        add(f"ffn{layer}", 4 * (FC // 2))
        for p in range(4):
            add(f"down{layer}{p}", len(panel_slots(FC)))
    return table, n


STAGES, N_SLOTS = stage_table()


def t5_bucket(dist):
    exact = N_BUCKETS // 2
    dd = np.maximum(dist, 1).astype(np.float64)
    large = exact + (np.log(dd / exact) / np.log(REL_MAX / exact) * (N_BUCKETS - exact)).astype(np.int32)
    return np.where(dist < exact, dist, np.minimum(large, N_BUCKETS - 1)).astype(np.int32)


F_LEN = 640
SKEW = F_LEN + P


def distance_select():
    sel = np.zeros((N_BUCKETS + 1, 3, F_LEN), np.float32)
    for g, (window, dil) in enumerate(DIL):
        reach = 255 if g == 0 else 511
        for x in range(F_LEN):
            d = reach - x
            if 0 <= d <= window and d % dil == 0:
                sel[t5_bucket(np.array([d]))[0], g, x] = 1.0
            else:
                sel[N_BUCKETS, g, x] = NEG
    return sel


C_IDENT, C_ONE, C_ZERO, C_KEEP, C_DROP, C_TRI, C_ONES = 0, 128, 129, 130, 258, 386, 514
C_N = 642
M_RESET, M_SEL, M_SAME, M_CAUSAL, M_WAUP = 0, 512, 1024, 1152, 1280
M_N = 1536


def constants():
    c = np.zeros((P, C_N), np.float32)
    r = np.arange(P)
    c[:, C_IDENT:C_IDENT + P] = np.eye(P)
    c[:, C_ONE] = 1.0
    c[:, C_KEEP:C_KEEP + P] = r[:, None] < r[None, :]
    c[:, C_DROP:C_DROP + P] = r[:, None] >= r[None, :]
    c[:, C_TRI:C_TRI + P] = -(r[:, None] >= r[None, :]).astype(np.float32)
    c[:, C_ONES:C_ONES + P] = -1.0
    m = np.zeros((P, M_WAUP), np.float32)
    m[:, M_RESET:M_RESET + S] = (np.arange(S) % CHUNK != 0)[None, :]
    for h in range(4):
        m[h, M_SEL + h * P:M_SEL + (h + 1) * P] = 1.0
    m[:, M_SAME:M_SAME + P] = (r[:, None] // CHUNK == r[None, :] // CHUNK) & (r[:, None] <= r[None, :])
    m[:, M_CAUSAL:M_CAUSAL + P] = np.where(r[:, None] <= r[None, :], 0.0, NEG)
    return c, m


V_C = 0
V_ADAB = V_C + KC
V_LNG = V_ADAB + 96
V_LNB = V_LNG + 32
V_BA = V_LNB + 32
V_GN = V_BA + 2
V_CW = V_GN + KC
V_CB = V_CW + 32
V_BI = V_CB + KC
V_BF = V_BI + 1
V_N = V_BF + 1

OFS = (0, 512, 1024, 896)
WID = tuple(S - P * j for j in range(TB))
SC = 1280


def build_program(nc, wstream, astream, xT, vecs, const, const0, wa_up, dsel, rel, ln_rows, out):
    ctx = ExitStack()
    sems = {}

    def sem(name):
        if name not in sems:
            sems[name] = ctx.enter_context(nc.semaphore(name))
        return sems[name]

    place = [16512]

    def at(name, shape, dt=F32, offset=None):
        size = int(np.prod(shape[1:])) * 4
        size = (size + 31) // 32 * 32
        if offset is None:
            offset = place[0]
            place[0] += size
        return nc.alloc_sbuf_tensor_at(name, shape, dt, offset=offset)

    xa = at("xa", [P, KC, S])
    hi_at = place[0]
    h_hi = at("h_hi", [P, KC, S], F32R)
    h_lo = at("h_lo", [P, KC, S], F32R)
    raw = at("raw", [P, RAW, SLOT])
    w_hi = at("w_hi", [P, RING, SLOT], F32R)
    w_lo = at("w_lo", [P, RING, SLOT], F32R)
    ada_raw = at("ada_raw", [P, 2, SLOT])
    ada_acc = at("ada_acc", [P, SLOT])
    tmp = at("tmp", [P, 2, S])
    cst = at("cst", [P, C_N])
    vec = at("vec", [P, V_N])
    c_act = at("c_act", [P, KC])
    mod = at("mod", [P, 12, KC])
    scl = at("scl", [P, 4, KC])
    bia = at("bia", [P, 4, KC])
    gate1 = at("gate1", [P, 4, KC])
    lnga = at("lnga", [P, 4, KC])
    lnba = at("lnba", [P, 4, KC])
    stats = at("stats", [P, 16, 6])
    mv = at("mv", [P, 16, 2])
    rstd = at("rstd", [P, 16])
    stats2 = at("stats2", [P, 16, 6])
    mv2 = at("mv2", [P, 16, 2])
    cols = at("cols", [P, 6, 16])
    vec_eps = at("vec_eps", [P, 1])
    arena = place[0]
    assert arena + 22528 * 4 <= 229344, arena

    def ar(name, shape, col, dt=F32):
        assert arena + (col + int(np.prod(shape[1:]))) * 4 <= 229344, (name, arena)
        return at(name, shape, dt, offset=arena + 4 * col)

    hid_hi = ar("hid_hi", [P, FC, S], 0, F32R)
    hid_lo = ar("hid_lo", [P, FC, S], FC * S, F32R)
    xh = ar("xh", [P, TB, D], 0)
    rt_mixer = ar("rt_mixer", [P, TB, D], 4096)
    rt_ffn = at("rt_ffn", [P, TB, D], offset=hi_at)
    ada_first = ar("ada_first", [P, 16, SLOT], 0)
    x_in = ar("x_in", [P, KC, S], 16384)
    rows_gb = at("rows_gb", [P, 2, D], offset=hi_at + KC * S * 4)
    og = ar("og", [P, TB, D], 0)
    va = ar("va", [P, TB, S], 4096)
    vb = ar("vb", [P, TB, 4, 129], 6144)
    qk = ar("qk", [P, KC, S], 8208)
    q_in = ar("q_in", [P, 2, S], 12304)
    k_in = ar("k_in", [P, 2, S], 13328)
    kdt = ar("kdt", [P, TB, 2, P], 14352)
    st = ar("st", [P, 2, 8, P], 15376)
    rows = ar("rows", [4, 4, S], 15376)
    ml_w = ar("ml_w", [P, 2, SC], 12304)
    ml_a = ar("ml_a", [P, 2, SC], 14864)
    scan_b = ar("scan_b", [P, S], 17424)
    t1 = ar("t1", [P, S], 17936)
    t2 = ar("t2", [P, S], 18448)
    a_low = ar("a_low", [16, S], 18960)
    gla_p = ar("gla_p", [P, 4, S], 17424)
    num = ar("num", [P, 4, TB, 129], 17424)
    neg_g = ar("neg_g", [4, S], 19488)
    q_raw = ar("q_raw", [P, 2, 515], 20000)
    dec = ar("dec", [P, 2, NCH], 21040)
    mcon = ar("mcon", [P, M_N], 23008 - M_N)
    a_col, em_col = cols[:, 0, :], cols[:, 1, :]
    qc = ar("qc", [P, 4, S], 0)
    kc = ar("kc", [P, 4, S], 2048)
    vc = ar("vc", [P, TB, S], 4096)
    qd = ar("qd", [P, 6, S], 6144)
    kd = ar("kd", [P, 6, S], 9216)
    vd = ar("vd", [P, TB, 768], 12288)
    sb_a = [ar(f"sb_a{i}", [P, SC], 15360 + 2560 * i) for i in range(2)]
    sb_sp = [ar(f"sb_sp{i}", [P, SC], 16640 + 2560 * i) for i in range(2)]
    strip = [ar(f"strip{h}", [P, SC], 20480 if h == 0 else SC * (h - 1)) for h in range(4)]
    od = ar("od", [P, TB, 256], 21760)
    f_rows = ar("f_rows", [4, 3, F_LEN], 17920)
    sel_sb = ar("sel_sb", [33, 3, F_LEN], 15360)
    rel_sb = ar("rel_sb", [33, 12], 17400)
    f_dram = nc.dram_tensor("f_scratch", (12, F_LEN), F32, kind="Internal").ap()
    skew = nc.dram_tensor("skew_scratch", (12, P, SKEW), F32, kind="Internal").ap()
    lg = [ar(f"lg{i}", [P, SC], 15360 + SC * i) for i in range(2)]
    pt = [ar(f"pt{i}", [P, SC], 17920 + SC * i) for i in range(2)]
    den, mx0, mx1 = cols[:, 2, :], cols[:, 3, :], cols[:, 4, :]

    ps = ctx.enter_context(nc.psum_tensor("ps", [P, 8, S], F32))
    psf = ps[:].rearrange("p b n -> p (b n)")
    ident = cst[:, C_IDENT:C_IDENT + P]
    one_col = cst[:, C_ONE:C_ONE + 1]
    zero_col = cst[:, C_ZERO:C_ZERO + 1]

    full_count = [0]
    uses = []
    where = {}

    def use(name, free, last_slot=None, own=1):
        i = len(uses)
        full = []
        for b in range(2):
            if b < own or last_slot is None:
                full_count[0] += 1
                full.append(("bank_full", full_count[0]))
            else:
                full.append(("slot_done", last_slot + 1))
        uses.append((i % 2, full, free))
        where[name] = i

    def last(name):
        first, n = STAGES[name]
        return first + n - 1

    use("narrow", [("low_ready", 1), ("row_step", 3)], 0)
    use("qa", [("prep_dve", 13)], last("qa"))
    use("ka", [("prep_dve", 16)], last("ka"))
    V_FREE = {"va": 0, "vb": 1, "vc": 2, "vd0": 3, "vd1": 4}

    def group(name, free0, free1):
        use(name, free0, last(name), own=2)
        use(name + "+", free1, last(name))

    def vgroup(name):
        i = V_FREE[name]
        group(name, [("v_act", 2 * i + 1), ("v_dve", 2 * i + 1)], [("v_act", 2 * i + 2), ("v_dve", 2 * i + 2)])

    vgroup("va")
    for p in range(4):
        use(f"qkb{p}", [("conv_in", 2 * p + 2)], last(f"qkb{p}"))
    vgroup("vb")
    group("ra", [("ra_ready", 2)], [("ra_ready", 4)])
    group("ob", [("ob_ready", 2)], [("ob_ready", 4)])
    for norm in range(4):
        layer = norm // 2
        if norm % 2 == 0:
            if layer == 1:
                for i, (name, panels) in enumerate((("qc", 2), ("kc", 2), ("qd", 3), ("kd", 3))):
                    base = (0, 2, 4, 7)[i]
                    for p in range(panels):
                        e = base + p
                        use(f"{name}{p}", [("qk1_act", e + 1), ("qk1_dve", e + 1)], last(f"{name}{p}"))
                vgroup("vc")
                vgroup("vd0")
                vgroup("vd1")
            down = [f"out{layer}{p}" for p in range(4)]
        else:
            for j in range(FC // 2):
                use(f"gate{layer}_{j}", [("silu_ready", FC * layer + 2 * j + 2)], STAGES[f"ffn{layer}"][0] + 4 * j + 1)
                use(f"up{layer}_{j}", [("prod_ready", FC * layer + 2 * j + 2)], STAGES[f"ffn{layer}"][0] + 4 * j + 3)
            down = [f"down{layer}{p}" for p in range(4)]
        for p, name in enumerate(down):
            use(name, [("r_ready", KC * norm + 2 * p + 2)], last(name))
        if norm < 3:
            for p in range(4):
                use(f"norm{norm}_{p}", [("xa_ready", KC * (norm + 1) + 2 * p + 2)])

    def pair(name):
        return 2 * uses[where[name]][0]

    def wait_full(eng, name, b):
        s, v = uses[where[name]][1][b]
        eng.wait_ge(sem(s), v)

    def wait_pair(eng, name):
        i = where[name]
        if i >= 2:
            for s, v in uses[i - 2][2]:
                eng.wait_ge(sem(s), v)

    def wait_free(eng, name):
        for s, v in uses[where[name]][2]:
            eng.wait_ge(sem(s), v)

    H_BASE = {"in": 0, "cat0": 8, "norm0": 16, "norm1": 24, "cat1": 32, "norm2": 38}



    def tile_of(n, width=P):
        return slice(n * width, (n + 1) * width)


    eps_col = vec_eps[:]
    GLA_BANK = (4, 5, 6, 4)
    KV_BANK = (4, 5, 4, 5, 6, 5, 6)
    NG_BANK = (3, 6)
    SB_COL = (0, 3 * S)

    v_dst = {
        "va": lambda tb: va[:, tb, :],
        "vb": lambda tb: vb[:, tb, :, 0:P],
        "vc": lambda tb: vc[:, tb, :],
        "vd0": lambda tb: vd[:, tb, 0:S],
        "vd1": lambda tb: vd[:, tb, S:768],
    }

    def v_src(name, tb):
        part, b = (name, tb) if tb < 2 else (name + "+", tb - 2)
        bank = ps[:, pair(part) + b, :]
        if name == "vb":
            return bank.rearrange("q (h d) -> q h d", h=4)
        return bank[:, 0:256] if name == "vd1" else bank

    def dil_tiles(t):
        return [(1, j) for j in range(t + 1)] + [(2, j) for j in range(t + 1)] + [(0, j) for j in range(max(0, t - 1), t + 1)]

    def dil_cols(t):
        return P * len(dil_tiles(t))

    def rounds(i):
        per = [-(-len(dil_tiles(t)) // 4) for t in range(TB)]
        h, t = divmod(i, TB)
        n0 = h * sum(per) + sum(per[:t])
        n = len(dil_tiles(t))
        return [(n0 + r, 4 * r, min(n, 4 * r + 4)) for r in range(per[t])]

    def skew_rows(eng):
        eng.dma_start(bass.AP(skew.tensor, 0, [[P * SKEW, 12], [SKEW + 1, P], [1, F_LEN]]),
                      bass.AP(f_dram.tensor, 0, [[F_LEN, 12], [0, P], [1, F_LEN]])).then_inc(sem("skewed"), 16)

    def load_strip(eng, h):
        for i, g in enumerate((1, 2, 0)):
            n = 256 if g == 0 else S
            eng.dma_start(strip[h][:, i * S:i * S + n], skew[h * 3 + g, :, P - 1:P - 1 + n]).then_inc(sem(f"strip{h}"), 16)

    def turn_out(pe, i, p):
        for n in (2 * p, 2 * p + 1):
            pe.wait_ge(sem("r_ready"), KC * i + n + 1)
            if n >= 2:
                pe.wait_ge(sem("rt_ready"), KC * i + n - 1)
            for tb in range(TB):
                m = pe.transpose(ps[:, 4 + n % 2, tile_of(tb)], xa[:, n, tile_of(tb)], ident)
            m.then_inc(sem("rt_full"), 1)

    block = ctx.enter_context(nc.Block())

    ADA_AFTER = {18: 2, 22: 3, 26: 4, 30: 5}

    @block.sync
    def _(sp):
        sp.dma_start(vec[:], vecs).then_inc(sem("in_vec"), 16)
        for q in range(4):
            sp.dma_start(ada_first[:, 4 * q:4 * q + 4, :],
                         astream[4 * q:4 * q + 4].rearrange("s p n -> p s n")).then_inc(sem(f"in_ada{q}"), 16)
            if q == 1:
                sp.dma_start(cst[:], const).then_inc(sem("in_const"), 16)
                sp.dma_start(x_in[:], xT.rearrange("(k p) t -> p k t", p=P)).then_inc(sem("in_x"), 16)
        sp.dma_start(mcon[:, 0:M_WAUP], const0).then_inc(sem("in_mcon"), 16)
        sp.dma_start(mcon[0:16, M_WAUP:M_N], wa_up).then_inc(sem("in_mcon"), 16)

        def load(s):
            if s >= RAW:
                sp.wait_ge(sem("w_lo_ready"), s - RAW + 1)
            sp.dma_start(raw[:, s % RAW, :], wstream[s]).then_inc(sem(f"raw_landed{s % RAW}"), 16)

        def load_ada(i):
            if i >= 18:
                sp.wait_ge(sem("ada_step"), i - 1)
            sp.dma_start(ada_raw[:, i % 2, :], astream[i]).then_inc(sem(f"ada_landed{i % 2}"), 16)

        s0 = STAGES["ffn0"][0]
        for s in range(s0 + 4):
            load(s)
            if s in ADA_AFTER:
                for k in range(KC):
                    load_ada(KC * ADA_AFTER[s] + k)

        with sp.Fori(1, FC // 2) as j:
            for u in range(4):
                sp.wait_ge(sem("w_lo_ready"), 4 * j + (s0 + u - RAW + 1))
                sp.dma_start(raw[:, (s0 + u) % RAW, :], wstream[bass.ds(4 * j + (s0 + u), 1)].rearrange("s p n -> p (s n)")
                             ).then_inc(sem(f"raw_landed{(s0 + u) % RAW}"), 16)
                sp.wait_ge(sem("ada_step"), 4 * j + (44 + u - 1))
                sp.dma_start(ada_raw[:, u % 2, :], astream[bass.ds(4 * j + (44 + u), 1)].rearrange("s p n -> p (s n)")
                             ).then_inc(sem(f"ada_landed{u % 2}"), 16)
        for s in range(s0 + 44, s0 + 44 + 6):
            load(s)
        for k in range(KC):
            load_ada(KC * 11 + k)
        first = STAGES["qc0"][0] + RING
        for s in range(s0 + 50, first):
            load(s)
        sp.wait_ge(sem("xh_ready"), 2 * TB)
        sp.dma_start(sel_sb[:], dsel).then_inc(sem("in_sel"), 16)
        sp.dma_start(rel_sb[:], rel).then_inc(sem("in_sel"), 16)
        s1 = STAGES["ffn1"][0]
        for s in range(first, s1 + 4):
            load(s)
        with sp.Fori(1, FC // 2) as j:
            for u in range(4):
                sp.wait_ge(sem("w_lo_ready"), 4 * j + (s1 + u - RAW + 1))
                sp.dma_start(raw[:, (s1 + u) % RAW, :], wstream[bass.ds(4 * j + (s1 + u), 1)].rearrange("s p n -> p (s n)")
                             ).then_inc(sem(f"raw_landed{(s1 + u) % RAW}"), 16)
        for s in range(s1 + 44, s1 + 52):
            load(s)
        sp.wait_ge(sem("slot_done"), s1 + 44)
        sp.dma_start(rows_gb[:], ln_rows).then_inc(sem("in_rows"), 16)
        for s in range(s1 + 52, N_SLOTS):
            load(s)
        for tb in range(TB):
            sp.wait_ge(sem("out_ready"), tb + 1)
            sp.dma_start(out[tile_of(tb), :], xh[:, tb, :]).then_inc(sem("stored"), 16)
        sp.wait_ge(sem("stored"), 16 * TB)

    @block.gpsimd
    def _(pool):
        def split(s, slot):
            pool.wait_ge(sem("w_hi_ready"), s + 1)
            nc.gpsimd.tensor_tensor(w_lo[:, slot, :], raw[:, slot % RAW, :], w_hi[:, slot, :].bitcast(F32),
                                    ALU.subtract).then_inc(sem("w_lo_ready"), 1)

        assert RAW == RING
        with pool.Fori(0, N_SLOTS // RING) as i:
            for u in range(RING):
                split(RING * i + u, u)
        for s in range(N_SLOTS // RING * RING, N_SLOTS):
            split(s, s % RING)

    @block.scalar
    def _(act):
        done = [0]

        def to_hi(s, slot, wait_free=True):
            act.wait_ge(sem(f"raw_landed{slot}"), 16 + 16 * (s // RAW) if isinstance(s, int) else 4 * s + (16 - 4 * slot))
            if wait_free:
                act.wait_ge(sem("slot_done"), s - RING + 1)
            nc.scalar.activation(w_hi[:, slot, :], raw[:, slot, :], ACT.Copy).then_inc(sem("w_hi_ready"), 1)

        def hi_until(n):
            for s in range(done[0], min(n, N_SLOTS)):
                to_hi(s, s % RING, s >= RING)
            done[0] = max(done[0], min(n, N_SLOTS))

        def ahead(name):
            hi_until(STAGES[name][0] + STAGES[name][1] + RING - 1)

        def hi_of_chunk(e, n):
            act.wait_ge(sem("h_tmp_ready"), e + 1)
            nc.scalar.activation(h_hi[:, n, :], tmp[:, e % 2, :], ACT.Copy).then_inc(sem("h_hi_ready"), 1)

        hi_until(RING)
        act.wait_ge(sem("in_vec"), 16)
        nc.scalar.activation(c_act[:], vec[:, V_C:V_C + KC], ACT.Silu).then_inc(sem("c_ready"), 1)
        act.wait_ge(sem("in_x"), 16)
        for n in range(KC):
            nc.scalar.activation(xa[:, n, :], x_in[:, n, :], ACT.Copy, scale=ALPHA).then_inc(sem("xa_ready"), 1)
        for n in range(KC):
            hi_of_chunk(H_BASE["in"] + n, n)

        ahead("narrow")
        wait_full(act, "narrow", 0)
        nc.scalar.activation(a_low[:], ps[0:16, pair("narrow"), :], ACT.Copy).then_inc(sem("low_ready"), 1)
        act.wait_ge(sem("row_step"), 2)
        nc.scalar.activation(rows[:, 1, :], rows[:, 1, :], ACT.Exp).then_inc(sem("row_act"), 1)
        act.wait_ge(sem("row_act"), 1)
        nc.scalar.activation(rows[:, 1, :], rows[:, 1, :], ACT.Ln, bias=1.0).then_inc(sem("row_act"), 1)
        for p in range(2):
            a0, d0 = 6 * p, 8 * p
            step = sem("prep_act")
            act.wait_ge(sem("prep_dve"), d0 + 2)
            nc.scalar.activation(t1[:], t1[:], ACT.Exp).then_inc(step, 1)
            act.wait_ge(step, a0 + 1)
            nc.scalar.activation(t1[:], t1[:], ACT.Ln, bias=1.0).then_inc(step, 1)
            act.wait_ge(sem("prep_dve"), d0 + 4)
            nc.scalar.activation(t1[:], scan_b[:], ACT.Exp, scale=1 / TAU).then_inc(step, 1)
            nc.scalar.activation(dec[:, p, :], scan_b[:, CHUNK - 1::CHUNK], ACT.Exp, scale=1 / TAU).then_inc(step, 1)
            if p == 0:
                ahead("qa")
            act.wait_ge(sem("prep_dve"), d0 + 5)
            nc.scalar.activation(t1[:], scan_b[:], ACT.Exp, scale=-1 / TAU).then_inc(step, 1)
            act.wait_ge(sem("prep_dve"), d0 + 6)
            nc.scalar.activation(t2[:], t2[:], ACT.Exp, scale=1 / TAU).then_inc(step, 1)
            if p == 0:
                ahead("ka")
        act.wait_ge(sem("am_copied"), 1)
        nc.scalar.activation(em_col, ps[:, 6, 16:32], ACT.Exp, scale=-1.0).then_inc(sem("em_ready"), 1)

        def v_blocks(name, dst):
            for tb in (0, 2):
                part = name if tb == 0 else name + "+"
                wait_full(act, part, 0)
                nc.scalar.activation(dst(tb), v_src(name, tb), ACT.Copy).then_inc(sem("v_act"), 1)

        ahead("va")
        v_blocks("va", v_dst["va"])
        for p in range(2):
            act.wait_ge(sem("kd_full"), p + 1)
            nc.scalar.activation(kdt[:, :, p, :], ps[:, 4 + p, :].rearrange("q (t d) -> q t d", t=TB), ACT.Copy
                                 ).then_inc(sem("kd_ready"), 1)

        for p in range(4):
            name = f"qkb{p}"
            ahead(name)
            for b in range(2):
                ch = 2 * p + b
                wait_full(act, name, b)
                if ch >= 2:
                    act.wait_ge(sem("conv_done"), ch - 1)
                else:
                    act.wait_ge(sem("pads_ready"), 1)
                nc.scalar.activation(q_raw[:, b, 3:3 + S], ps[:, pair(name) + b, :], ACT.Copy).then_inc(sem("conv_in"), 1)
            for b in range(2):
                ch = 2 * p + b
                act.wait_ge(sem("conv_done"), ch + 1)
                nc.scalar.activation(qk[:, ch, :], tmp[:, b, :], ACT.Silu).then_inc(sem("qk_ready"), 1)

        ahead("vb")
        v_blocks("vb", v_dst["vb"])
        for name, func, col in (("ra", ACT.Silu, 0), ("ob", ACT.Sigmoid, S)):
            ahead(name)
            for tb in range(TB):
                part, b = (name, tb) if tb < 2 else (name + "+", tb - 2)
                wait_full(act, part, b)
                nc.scalar.activation(og[:, tb, col:col + S], ps[:, pair(part) + b, :], func).then_inc(sem(f"{name}_ready"), 1)
            if name == "ra":
                act.wait_ge(sem("o_done"), TB)
                nc.scalar.activation(cols[:, 5, :], mv[:, :, 1], ACT.Sqrt, bias=eps_col).then_inc(sem("std_gla"), 1)

        def ml_weights(h):
            act.wait_ge(sem("ed_ready"), h + 1)
            if h == 0:
                act.wait_ge(sem("pv_free"), 1)
            if h >= 2:
                act.wait_ge(sem("ml_a_ready"), h - 1)
            for j in range(TB):
                bias = a_col[:, j * 4 + h:j * 4 + h + 1]
                i = nc.scalar.activation(ml_w[:, h % 2, OFS[j]:OFS[j] + P], tmp[:, h % 2, tile_of(j)], ACT.Exp, bias=bias)
                if j < TB - 1:
                    i = nc.scalar.activation(ml_w[:, h % 2, OFS[j] + P:OFS[j] + WID[j]],
                                             ps[:, NG_BANK[h % 2], (j + 1) * P:S], ACT.Exp, bias=bias)
            i.then_inc(sem("ml_w_ready"), 1)

        def ml_out(h):
            act.wait_ge(sem("num_full"), h + 1)
            for b in range(2):
                i = nc.scalar.activation(num[:, h, 2 * b:2 * b + 2, :],
                                         ps[:, 4 + b, 0:258].rearrange("q (t d) -> q t d", t=2), ACT.Copy)
            i.then_inc(sem("num_ready"), 1)

        ml_weights(0)
        ml_weights(1)
        for h in range(4):
            ml_out(h)
            if h + 2 < 4:
                ml_weights(h + 2)
        act.wait_ge(sem("num_ready"), 4)
        nc.scalar.activation(cols[:, 2, :], num[:, :, :, 128].rearrange("q h t -> q (h t)"), ACT.Abs).then_inc(sem("den_abs"), 1)
        act.wait_ge(sem("ml_var"), 1)
        nc.scalar.activation(cols[:, 4, :], cols[:, 4, :], ACT.Sqrt, bias=eps_col).then_inc(sem("ml_std"), 1)
        for n in range(KC):
            hi_of_chunk(H_BASE["cat0"] + n, n)

        def norm(i, names, rt):
            for n in range(KC):
                ahead(names[n // 2])
                act.wait_ge(sem("rt_full"), KC * i + n + 1)
                nc.scalar.activation(rt[:, :, tile_of(n)], ps[:, 4 + n % 2, :].rearrange("q (t d) -> q t d", t=TB),
                                     ACT.Copy).then_inc(sem("rt_ready"), 1)
            act.wait_ge(sem("mv_ready"), i + 1)
            nc.scalar.activation(cols[:, 5, 0:TB], mv[:, 0:TB, 1], ACT.Sqrt, bias=eps_col).then_inc(sem("std_ready"), 1)
            if i == 3:
                return
            for n in range(KC):
                hi_of_chunk(H_BASE[f"norm{i}"] + n, n)
                nc.scalar.activation(xa[:, n, :], ps[:, pair(f"norm{i}_{n // 2}") + n % 2, :], ACT.Identity,
                                     scale=lnga[:, i, n:n + 1], bias=lnba[:, i, n:n + 1]).then_inc(sem("xa_ready"), 1)

        def ffn(layer):
            s0 = STAGES[f"ffn{layer}"][0]
            f0 = uses[where[f"gate{layer}_0"]][1][0][1]
            gate = pair(f"gate{layer}_0")

            def step(j, first=False):
                for s in (3, 4):
                    to_hi(4 * j + (s0 + s), (s0 + s) % RING)
                for b in range(2):
                    act.wait_ge(*((sem("bank_full"), 2 * j + f0) if b == 0 else (sem("slot_done"), 4 * j + (s0 + 2))))
                    if first:
                        act.wait_ge(sem("h_ready"), H_BASE[f"norm{2 * layer}"] + KC)
                    else:
                        act.wait_ge(sem("hid_ready"), 2 * j + (FC * layer - 1 + b))
                    nc.scalar.activation(tmp[:, b, :], ps[:, gate + b, :], ACT.Silu).then_inc(sem("silu_ready"), 1)
                for s in (5, 6):
                    to_hi(4 * j + (s0 + s), (s0 + s) % RING)
                for b in range(2):
                    act.wait_ge(sem("prod_ready"), 2 * j + (FC * layer + 1 + b))
                    dst = hid_hi[:, b, :] if first else hid_hi[:, bass.ds(2 * j + b, 1), :].rearrange("p o t -> p (o t)")
                    nc.scalar.activation(dst, tmp[:, b, :], ACT.Copy).then_inc(sem("hid_hi_ready"), 1)

            hi_until(s0 + 3)
            step(0, True)
            with act.Fori(1, FC // 2) as j:
                step(j)
            done[0] = s0 + 4 * (FC // 2) + 3

        norm(0, [f"out0{p}" for p in range(4)], rt_mixer)
        ffn(0)
        norm(1, [f"down0{p}" for p in range(4)], rt_ffn)

        for name, dst, panels, scale in (("qc", qc, 2, 0.125), ("kc", kc, 2, 1.0), ("qd", qd, 3, 0.125), ("kd", kd, 3, 1.0)):
            for p in range(panels):
                part = f"{name}{p}"
                ahead(part)
                wait_full(act, part, 0)
                nc.scalar.activation(dst[:, 2 * p, :], ps[:, pair(part), :], ACT.Copy, scale=scale).then_inc(sem("qk1_act"), 1)
            if name == "kc":
                act.wait_ge(sem("f_ready"), 1)
                act.dma_start(f_dram.rearrange("(h g) x -> h g x", h=4), f_rows[:]).then_inc(sem("f_stored"), 16)
            if name == "qd":
                act.wait_ge(sem("f_stored"), 16)
                skew_rows(act)
            if name == "kd":
                act.wait_ge(sem("skewed"), 16)
                load_strip(act, 0)
        for name in ("vc", "vd0", "vd1"):
            ahead(name)
            v_blocks(name, v_dst[name])

        def sb_first(h):
            z = psf[:, SB_COL[h % 2]:SB_COL[h % 2] + SC]
            a = sb_a[h % 2]
            act.wait_ge(sem("z_full"), h + 1)
            if h >= 2:
                act.wait_ge(sem("av_done"), h - 1)
            nc.scalar.activation(a[:], z, ACT.Abs).then_inc(sem("sb_act"), 1)
            act.wait_ge(sem("sb_act"), 3 * h + 1)
            nc.scalar.activation(a[:], a[:], ACT.Exp, scale=-1.0).then_inc(sem("sb_act"), 1)
            act.wait_ge(sem("sb_act"), 3 * h + 2)
            nc.scalar.activation(a[:], a[:], ACT.Ln, bias=1.0).then_inc(sem("sb_act"), 1)

        def sb_second(h):
            act.wait_ge(sem("tri_full"), h + 1)
            nc.scalar.activation(sb_a[h % 2][:], psf[:, SB_COL[h % 2]:SB_COL[h % 2] + SC], ACT.Exp).then_inc(sem("att_exp"), 1)

        sb_first(0)
        for h in range(8):
            if h + 1 < 8:
                sb_first(h + 1)
            sb_second(h)
            if h % 2 == 0 and h >= 2:
                hi_of_chunk(H_BASE["cat1"] + h // 2 - 1, h // 2 - 1)
        hi_of_chunk(H_BASE["cat1"] + 3, 3)
        for h in (1, 2, 3):
            load_strip(act, h)

        def dil_exp(i):
            h, t = divmod(i, TB)
            n = dil_cols(t)
            act.wait_ge(sem("dil_max"), i + 1)
            nc.scalar.activation(lg[i % 2][:, 0:n], lg[i % 2][:, 0:n], ACT.Exp, bias=mx1[:, i:i + 1],
                                 accum_out=den[:, i:i + 1]).then_inc(sem("dil_p"), 1)

        def dil_turn(i):
            for r in rounds(i):
                act.wait_ge(sem("turn_full"), r[0] + 1)
                if r[1] == 0 and i >= 2:
                    act.wait_ge(sem("pv_done"), i - 1)
                nc.scalar.activation(pt[i % 2][:, r[1] * P:r[2] * P], ps[:, 6, 0:(r[2] - r[1]) * P], ACT.Copy
                                     ).then_inc(sem("turn_ready"), 1)

        dil_exp(0)
        for i in range(4 * TB):
            if i + 1 < 4 * TB:
                dil_exp(i + 1)
            dil_turn(i)
        for n in range(4, 6):
            hi_of_chunk(H_BASE["cat1"] + n, n)
        norm(2, [f"out1{p}" for p in range(4)], rt_mixer)
        ffn(1)
        norm(3, [f"down1{p}" for p in range(4)], rt_ffn)

    @block.tensor
    def _(pe):
        def slot_waits(s):
            pe.wait_ge(sem("w_hi_ready"), s + 1)
            pe.wait_ge(sem("w_lo_ready"), s + 1)

        def mm3(o, w_h, w_l, x_h, x_l, start, stop):
            pe.matmul(o, w_h, x_l, start=start, stop=False)
            pe.matmul(o, w_h, x_h, start=False, stop=False)
            return pe.matmul(o, w_l, x_h, start=False, stop=stop)

        def wpart(w, s, kk, b):
            return w[:, s % RING, kk * 256 + b * P:kk * 256 + (b + 1) * P]

        def panel(name, nk, x_h, x_l, ready=None):
            wait_pair(pe, name)
            first = STAGES[name][0]
            bank = pair(name)
            for i, (k0, n) in enumerate(panel_slots(nk)):
                s = first + i
                slot_waits(s)
                for b in range(2):
                    for kk in range(n):
                        k = k0 + kk
                        if ready and b == 0:
                            pe.wait_ge(sem(ready[0]), ready[1] + k + 1)
                        m = mm3(ps[:, bank + b, :], wpart(w_hi, s, kk, b), wpart(w_lo, s, kk, b), x_h[:, k, :], x_l[:, k, :],
                                k == 0, k == nk - 1)
                        if b == 0 and k == nk - 1:
                            m.then_inc(sem("bank_full"), 1)
                m.then_inc(sem("slot_done"), 1)

        def group(name, kk_n, width):
            first, count = STAGES[name]
            wait_pair(pe, name)
            for i in range(count):
                s = first + i
                slot_waits(s)
                for tb in range(TB):
                    part, b = (name, tb) if tb < 2 else (name + "+", tb - 2)
                    if i == 0 and tb == 2:
                        wait_pair(pe, part)
                    o = ps[:, pair(part) + b, 0:width]
                    for kk in range(kk_n):
                        k = i * kk_n + kk
                        w = slice(kk * width, (kk + 1) * width)
                        start, stop = k == 0, k == KC - 1
                        pe.matmul(o, h_lo[:, k, tile_of(tb)], w_hi[:, s % RING, w], start=start, stop=False)
                        pe.matmul(o, h_hi[:, k, tile_of(tb)], w_hi[:, s % RING, w], start=False, stop=False)
                        m = pe.matmul(o, h_hi[:, k, tile_of(tb)], w_lo[:, s % RING, w], start=False, stop=stop)
                    if i == count - 1 and tb < TB - 1:
                        m.then_inc(sem("bank_full"), 1)
                m.then_inc(sem("slot_done"), 1)

        def ada_cols(blk):
            pe.wait_ge(sem("ada_step"), KC * (blk + 1) if isinstance(blk, int) else KC * blk + KC)
            for n in range(KC):
                m = pe.matmul(ps[:, 7, n:n + 1], ada_acc[:, tile_of(n)], one_col, start=True, stop=True)
            m.then_inc(sem("ada_cols"), 1)

        pe.wait_ge(sem("in_const"), 16)
        ada_cols(0)
        pe.wait_ge(sem("mod_ready"), 1)
        ada_cols(1)

        slot_waits(0)
        for k in range(KC):
            pe.wait_ge(sem("h_ready"), H_BASE["in"] + k + 1)
            m = mm3(ps[0:96, 0, :], w_hi[:, 0, k * P:k * P + 96], w_lo[:, 0, k * P:k * P + 96], h_hi[:, k, :], h_lo[:, k, :],
                    k == 0, k == KC - 1)
        m.then_inc(sem("bank_full"), 1)
        pe.wait_ge(sem("in_mcon"), 32)
        pe.wait_ge(sem("low_ready"), 1)
        for p in range(2):
            m = pe.matmul(ps[:, 4 + p, :], mcon[0:16, M_WAUP + p * P:M_WAUP + (p + 1) * P], a_low[:], start=True, stop=True)
            if p == 0:
                m.then_inc(sem("slot_done"), 1)
        m.then_inc(sem("gate_full"), 1)
        panel("qa", KC, h_hi, h_lo)
        panel("ka", KC, h_hi, h_lo)
        pe.wait_ge(sem("row_step"), 4)
        for k, r in ((0, 0), (1, 2)):
            for tb in range(TB):
                m = pe.transpose(ps[:, 6, 16 * k + 4 * tb:16 * k + 4 * tb + 4], rows[:, r, tile_of(tb)], ident[0:4, 0:4])
        m.then_inc(sem("am_full"), 1)
        group("va", 2, S)
        for p in range(2):
            pe.wait_ge(sem("prep_dve"), 8 * p + 8)
            for tb in range(TB):
                m = pe.transpose(ps[:, 4 + p, tile_of(tb)], tmp[:, p, tile_of(tb)], ident)
            m.then_inc(sem("kd_full"), 1)
        panel("qkb0", KC, h_hi, h_lo)
        for h in range(4):
            p, e = divmod(h, 2)
            pe.wait_ge(sem("kd_ready"), 2) if h == 0 else None
            if h == 2:
                pe.wait_ge(sem("em_ready"), 1)
            if h == 3:
                pe.wait_ge(sem("gla_p_ready"), 1)
            for tb in range(TB):
                m = pe.matmul(ps[:, GLA_BANK[h], tile_of(tb)], k_in[64 * e:64 * e + 64, p, tile_of(tb)],
                              q_in[64 * e:64 * e + 64, p, tile_of(tb)], start=True, stop=True)
            m.then_inc(sem("gla_s_full"), 1)
        panel("qkb1", KC, h_hi, h_lo)

        def chunk_sums(p):
            for c in range(NCH - 1):
                if c == 0:
                    pe.wait_ge(*((sem("gla_p_ready"), 4) if p == 0 else (sem("st_ready"), 7)))
                if c == 5:
                    pe.wait_ge(sem("st_ready"), 7 * p + 4)
                if c == 0:
                    pe.wait_ge(sem("v_dve"), 2)
                r = 64 * (c % 2)
                m = pe.matmul(ps[:, KV_BANK[c], (c // 2 % 2) * 256:(c // 2 % 2) * 256 + 256], kdt[r:r + 64, c // 2, p, :],
                              va[r:r + 64, c // 2, p * 256:(p + 1) * 256], start=True, stop=True, skip_group_check=True)
                if c in (3, 6):
                    m.then_inc(sem("kv_full"), 1)

        chunk_sums(0)
        panel("qkb2", KC, h_hi, h_lo)
        chunk_sums(1)
        ada_cols(2)
        panel("qkb3", KC, h_hi, h_lo)
        group("vb", 2, S)
        ada_cols(3)
        group("ra", 2, S)
        pe.wait_ge(sem("st_ready"), 14)
        for tb in range(TB):
            if tb == 3:
                pe.wait_ge(sem("o_done"), 1)
            bank = GLA_BANK[tb]
            for h in range(4):
                pe.matmul(ps[:, bank, tile_of(h)], gla_p[:, h, tile_of(tb)], va[:, tb, tile_of(h)],
                          start=h == 0, stop=False, skip_group_check=True)
            for h in (0, 2, 1, 3):
                p, e = divmod(h, 2)
                if h == 1:
                    m.then_inc(sem("lower_done"), 1)
                    pe.wait_ge(sem("lower_done"), tb + 1)
                for c in (2 * tb, 2 * tb + 1):
                    if c:
                        r = 64 * (c % 2)
                        m = pe.matmul(ps[r:r + 64, bank, tile_of(h)], q_in[64 * e:64 * e + 64, p, c * CHUNK:(c + 1) * CHUNK],
                                      st[64 * e:64 * e + 64, p, c - 1, :], start=False, stop=True, skip_group_check=True)
            m.then_inc(sem("o_full"), 1)
        ada_cols(4)
        group("ob", 2, S)

        def neg_rows(h):
            if h >= 2:
                pe.wait_ge(sem("ml_w_ready"), h - 1)
            pe.matmul(ps[:, NG_BANK[h % 2], :], mcon[0:4, M_SEL + h * P:M_SEL + (h + 1) * P], neg_g[:],
                      start=True, stop=True).then_inc(sem("ng_full"), 1)

        def ml_scores(h):
            if h == 0:
                pe.wait_ge(sem("qk_ready"), KC)
            if h >= 1:
                pe.wait_ge(sem("ml_a_ready"), h)
            for j in range(TB):
                m = pe.matmul(psf[:, OFS[j]:OFS[j] + WID[j]], qk[:, 4 + h, tile_of(j)], qk[:, h, j * P:S],
                              start=True, stop=True, skip_group_check=True)
            m.then_inc(sem("ml_s_full"), 1)

        def ml_num(h):
            pe.wait_ge(sem("ml_a_ready"), h + 1)
            if h == 0:
                pe.wait_ge(sem("v_dve"), 4)
            if h >= 1:
                pe.wait_ge(sem("num_ready"), h)
            for tb in range(TB):
                o = ps[:, 4 + tb // 2, (tb % 2) * 129:(tb % 2) * 129 + 129]
                for j in range(tb + 1):
                    m = pe.matmul(o, ml_a[:, h % 2, OFS[j] + (tb - j) * P:OFS[j] + (tb - j + 1) * P], vb[:, j, h, :],
                                  start=j == 0, stop=j == tb, skip_group_check=True)
            m.then_inc(sem("num_full"), 1)

        wait_free(pe, "ob")
        wait_free(pe, "ob+")
        pe.wait_ge(sem("o_done"), TB)
        neg_rows(0)
        ml_scores(0)
        neg_rows(1)
        ml_scores(1)
        neg_rows(2)
        ml_num(0)
        ml_scores(2)
        neg_rows(3)
        ml_num(1)
        ml_scores(3)
        ml_num(2)
        ml_num(3)
        ada_cols(5)

        def turn_in(e, n, src, ready):
            pe.wait_ge(*ready)
            if n >= 2:
                pe.wait_ge(sem("h_tmp_ready"), e - 1)
            for tb in range(TB):
                m = pe.transpose(ps[:, 4 + n % 2, tile_of(tb)], src(tb), ident)
            m.then_inc(sem("cat_full"), 1)

        pe.wait_ge(sem("num_ready"), 4)
        for n in range(KC):
            turn_in(H_BASE["cat0"] + n, n, lambda tb: og[:, tb, tile_of(n)], (sem("og_ready"), 1 if n < 4 else 2))
        for p in range(4):
            panel(f"out0{p}", KC, h_hi, h_lo, ("h_ready", H_BASE["cat0"]) if p == 0 else None)
            turn_out(pe, 0, p)

        def turn_back(i):
            for n in range(KC):
                name = f"norm{i}_{n // 2}"
                if n % 2 == 0:
                    wait_pair(pe, name)
                for tb in range(TB):
                    if n == 0:
                        pe.wait_ge(sem("xh_ready"), TB * i + tb + 1)
                    m = pe.transpose(ps[:, pair(name) + n % 2, tile_of(tb)], xh[:, tb, tile_of(n)], ident)
                m.then_inc(sem("bank_full"), 1)

        def ffn(layer):
            s0 = STAGES[f"ffn{layer}"][0]
            i = where[f"gate{layer}_0"]

            def step(j, first=False):
                for m_ in range(2):
                    bank = pair(f"gate{layer}_0") if m_ == 0 else pair(f"up{layer}_0")
                    if first:
                        wait_pair(pe, f"gate{layer}_0" if m_ == 0 else f"up{layer}_0")
                    else:
                        pe.wait_ge(sem("silu_ready" if m_ == 0 else "prod_ready"), 2 * j + FC * layer)
                    for half in range(2):
                        u = 2 * m_ + half
                        s = s0 + u
                        slot_waits(4 * j + s)
                        for b in range(2):
                            for kk in range(4):
                                k = 4 * half + kk
                                if first and m_ == 0 and b == 0:
                                    pe.wait_ge(sem("h_ready"), H_BASE[f"norm{2 * layer}"] + k + 1)
                                m = mm3(ps[:, bank + b, :], wpart(w_hi, s, kk, b), wpart(w_lo, s, kk, b),
                                        h_hi[:, k, :], h_lo[:, k, :], k == 0, k == KC - 1)
                                if b == 0 and k == KC - 1:
                                    m.then_inc(sem("bank_full"), 1)
                        m.then_inc(sem("slot_done"), 1)

            assert uses[i][0] != uses[i + 1][0]
            step(0, True)
            if layer == 0:
                with pe.Fori(0, FC // 4) as it:
                    step(2 * it + 1)
                    step(2 * it + 2)
                    ada_cols(it + 6)
            else:
                with pe.Fori(1, FC // 2) as j:
                    step(j)
            for p in range(4):
                panel(f"down{layer}{p}", FC, hid_hi, hid_lo, ("hid_ready", FC * layer) if p == 0 else None)
                turn_out(pe, 2 * layer + 1, p)
                if layer == 0 and p == 1:
                    ada_cols(11)

        turn_back(0)
        ffn(0)
        turn_back(1)

        for name, panels in (("qc", 2), ("kc", 2), ("qd", 3), ("kd", 3)):
            for p in range(panels):
                panel(f"{name}{p}", KC, h_hi, h_lo, ("h_ready", H_BASE["norm1"]) if name == "qc" and p == 0 else None)
            if name == "qc":
                pe.wait_ge(sem("in_sel"), 32)
                pe.wait_ge(sem("mod_ready"), 12)
                for g in range(3):
                    pe.matmul(ps[0:4, (4, 6, 7)[g], :], rel_sb[:, 4 * g:4 * g + 4], sel_sb[:, g, 0:S], start=True, stop=True)
                    m = pe.matmul(ps[0:4, 5, g * P:(g + 1) * P], rel_sb[:, 4 * g:4 * g + 4], sel_sb[:, g, S:F_LEN],
                                  start=True, stop=True, skip_group_check=True)
                m.then_inc(sem("f_full"), 1)
        group("vc", 2, S)
        group("vd0", 2, S)
        group("vd1", 4, 256)

        def sb_z(h):
            c, r = h // 2, 64 * (h % 2)
            base = SB_COL[h % 2]
            if h >= 2:
                pe.wait_ge(sem("att_exp"), h - 1)
            for j in (0, 1, 2, 3):
                m = pe.matmul(psf[:, base + OFS[j]:base + OFS[j] + WID[j]], kc[r:r + 64, c, tile_of(j)], qc[r:r + 64, c, j * P:S],
                              start=j < 3, stop=False, skip_group_check=True)
            m.then_inc(sem("z_full"), 1)

        def sb_tri(h):
            base = SB_COL[h % 2]
            sp_ = sb_sp[h % 2]
            pe.wait_ge(sem("sp_ready"), h + 1)
            for j in range(TB):
                pe_out = psf[:, base + OFS[j]:base + OFS[j] + WID[j]]
                m = pe.matmul(pe_out, cst[:, C_TRI:C_TRI + P], sp_[:, OFS[j]:OFS[j] + WID[j]], start=False,
                              stop=j == TB - 1, skip_group_check=True)
                for k in range(j + 1, TB):
                    m = pe.matmul(psf[:, base + OFS[j] + (k - j) * P:base + OFS[j] + WID[j]], cst[:, C_ONES:C_ONES + P],
                                  sp_[:, OFS[k]:OFS[k] + WID[k]], start=False, stop=k == TB - 1, skip_group_check=True)
            m.then_inc(sem("tri_full"), 1)

        def sb_av(h):
            c, r = h // 2, 64 * (h % 2)
            pe.wait_ge(sem("att_ready"), h + 1)
            if h % 2 == 0 and h >= 4:
                pe.wait_ge(sem("h_tmp_ready"), H_BASE["cat1"] + c - 1)
            for j in range(TB):
                m = pe.matmul(ps[r:r + 64, 6 + c % 2, j * P:S], vc[:, j, h * 64:h * 64 + 64], sb_a[h % 2][:, OFS[j]:OFS[j] + WID[j]],
                              start=j == 0, stop=j == TB - 1, skip_group_check=True)
            m.then_inc(sem("av_done"), 1)

        wait_free(pe, "vd1")
        wait_free(pe, "vd1+")
        pe.wait_ge(sem("f_ready"), 1)
        sb_z(0)
        for h in range(8):
            if h + 1 < 8:
                sb_z(h + 1)
            if h >= 1:
                sb_av(h - 1)
            sb_tri(h)
        sb_av(7)

        def dil_qk(i):
            h, t = divmod(i, TB)
            r = 64 * (h % 2)
            if i >= 2:
                pe.wait_ge(sem("dil_max"), i - 1)
            base = 3 * (i % 2)
            for b, g in enumerate((1, 2, 0)):
                lo = max(0, t - 1) * P if g == 0 else 0
                hd = g * 4 + h
                m = pe.matmul(ps[:, base + b, 0:(t + 1) * P - lo], qd[r:r + 64, hd // 2, tile_of(t)],
                              kd[r:r + 64, hd // 2, lo:(t + 1) * P], start=True, stop=True)
            m.then_inc(sem("l_full"), 1)

        def dil_pv(i):
            h, t = divmod(i, TB)
            tiles = dil_tiles(t)
            pe.wait_ge(sem("dil_p"), i + 1)
            for n, b0, b1 in rounds(i):
                if n >= 1:
                    pe.wait_ge(sem("turn_ready"), n)
                for b in range(b0, b1):
                    m = pe.transpose(ps[:, 6, tile_of(b - b0)], lg[i % 2][:, tile_of(b)], ident)
                m.then_inc(sem("turn_full"), 1)
            if t == 0 and h >= 1:
                pe.wait_ge(sem("od_ready"), h)
            pe.wait_ge(sem("turn_ready"), rounds(i)[-1][0] + 1)
            for b, (g, key) in enumerate(tiles):
                hd = g * 4 + h
                m = pe.matmul(ps[:, 7, t * 64:t * 64 + 64], pt[i % 2][:, tile_of(b)], vd[:, key, hd * 64:hd * 64 + 64],
                              start=b == 0, stop=b == len(tiles) - 1, skip_group_check=True)
            m.then_inc(sem("pv_done"), 1)

        pe.wait_ge(sem("h_tmp_ready"), H_BASE["cat1"] + 4)
        pe.wait_ge(sem("att_exp"), 8)
        dil_qk(0)
        for i in range(4 * TB):
            if i + 1 < 4 * TB:
                dil_qk(i + 1)
            dil_pv(i)
        for n in range(4, 6):
            pe.wait_ge(sem("od_ready"), 4)
            for tb in range(TB):
                m = pe.transpose(ps[:, n, tile_of(tb)], od[:, tb, tile_of(n - 4)], ident)
            m.then_inc(sem("cat_full"), 1)
        for p in range(4):
            panel(f"out1{p}", 6, h_hi, h_lo, ("h_ready", H_BASE["cat1"]) if p == 0 else None)
            turn_out(pe, 2, p)
        turn_back(2)
        ffn(1)

    @block.vector
    def _(dve):
        chain = [0]
        V = nc.vector

        def link(ins):
            chain[0] += 1
            ins.then_inc(sem("dve_chain"), 1)
            dve.wait_ge(sem("dve_chain"), chain[0])

        def vcol(c, n=1):
            return vec[:, c:c + n]

        def lo_of_chunk(e, n):
            dve.wait_ge(sem("h_hi_ready"), e + 1)
            V.tensor_tensor(h_lo[:, n, :], tmp[:, e % 2, :], h_hi[:, n, :].bitcast(F32), ALU.subtract).then_inc(sem("h_ready"), 1)

        def tmp_free(e):
            if e >= 2:
                dve.wait_ge(sem("h_ready"), e - 1)

        def ada_slot(i, src, first):
            k = i % KC
            if first:
                if i:
                    dve.wait_ge(sem("ada_step"), i)
                V.tensor_scalar(ada_acc[:], src, c_act[:, k:k + 1], None, ALU.mult).then_inc(sem("ada_step"), 1)
            else:
                dve.wait_ge(sem("ada_step"), i)
                V.scalar_tensor_tensor(ada_acc[:], src, c_act[:, k:k + 1], ada_acc[:], ALU.mult, ALU.add
                                       ).then_inc(sem("ada_step"), 1)

        def mod_block(blk):
            dve.wait_ge(sem("ada_cols"), blk + 1)
            V.tensor_tensor(mod[:, blk, :], ps[:, 7, 0:KC], vcol(V_ADAB + blk * KC, KC), ALU.add).then_inc(sem("mod_ready"), 1)

        def ada_block(blk):
            if blk > 2:
                mod_block(blk - 1)
            for k in range(KC):
                i = KC * blk + k
                dve.wait_ge(sem(f"ada_landed{i % 2}"), 16 * ((i - 16) // 2 + 1))
                ada_slot(i, ada_raw[:, i % 2, :], k == 0)

        def derive(i, blk_shift, blk_scale, ln):
            if ln is None:
                V.tensor_scalar(scl[:, i, :], mod[:, blk_scale, :], 1.0, None, ALU.add)
                link(V.tensor_copy(bia[:, i, :], mod[:, blk_shift, :]))
                return
            V.scalar_tensor_tensor(scl[:, i, :], mod[:, blk_scale, :], 1.0, vcol(V_LNG + ln * KC, KC), ALU.add, ALU.mult)
            link(V.scalar_tensor_tensor(bia[:, i, :], mod[:, blk_scale, :], 1.0, vcol(V_LNB + ln * KC, KC), ALU.add, ALU.mult))
            link(V.tensor_tensor(bia[:, i, :], bia[:, i, :], mod[:, blk_shift, :], ALU.add))

        dve.wait_ge(sem("c_ready"), 1)
        for blk in range(2):
            if blk:
                mod_block(0)
            for k in range(KC):
                i = KC * blk + k
                dve.wait_ge(sem(f"in_ada{i // 4}"), 16)
                ada_slot(i, ada_first[:, i, :], k == 0)
        mod_block(1)
        dve.wait_ge(sem("mod_ready"), 2)
        derive(0, 0, 1, None)
        V.memset(eps_col, EPS)
        V.tensor_scalar(lnga[:], vcol(V_LNG, 32).rearrange("p (a b) -> p a b", a=4), ALPHA, None, ALU.mult)
        link(V.tensor_scalar(lnba[:], vcol(V_LNB, 32).rearrange("p (a b) -> p a b", a=4), ALPHA, None, ALU.mult))
        dve.wait_ge(sem("in_x"), 16)

        def chunk_from(e, n, src, i):
            tmp_free(e)
            V.tensor_scalar(tmp[:, e % 2, :], src, scl[:, i, n:n + 1], bia[:, i, n:n + 1], ALU.mult, ALU.add
                            ).then_inc(sem("h_tmp_ready"), 1)

        for n in range(KC):
            chunk_from(n, n, x_in[:, n, :], 0)
            if n >= 1:
                lo_of_chunk(n - 1, n - 1)
        lo_of_chunk(KC - 1, KC - 1)
        dve.wait_ge(sem("xa_ready"), KC)
        V.memset(q_raw[:, :, 0:3], 0.0).then_inc(sem("pads_ready"), 1)
        V.memset(vb[:, :, :, 128:129], 1.0)

        wait_full(dve, "narrow", 0)
        fps, ips = ps[64:68, 0, :], ps[32:36, 0, :]
        V.tensor_scalar(rows[:, 1, :], fps, vec[64:68, V_BF:V_BF + 1], 0.0, ALU.add, ALU.max)
        V.tensor_scalar(rows[:, 2, :], fps, vec[64:68, V_BF:V_BF + 1], 0.0, ALU.add, ALU.min).then_inc(sem("row_step"), 1)
        dve.wait_ge(sem("row_step"), 1)
        V.tensor_tensor(rows[:, 1, :], rows[:, 2, :], rows[:, 1, :], ALU.subtract).then_inc(sem("row_step"), 1)
        V.tensor_scalar(rows[:, 0, :], ips, vec[32:36, V_BI:V_BI + 1], None, ALU.add).then_inc(sem("row_step"), 1)
        prep = sem("prep_dve")

        def gla_gate(p):
            dve.wait_ge(sem("gate_full"), 1)
            if p == 1:
                dve.wait_ge(sem("prep_act"), 6)
                dve.wait_ge(prep, 8)
            g = ps[:, 4 + p, :]
            V.tensor_scalar(t1[:], g, vcol(V_BA + p), 0.0, ALU.add, ALU.max)
            V.tensor_scalar(t2[:], g, vcol(V_BA + p), 0.0, ALU.add, ALU.min).then_inc(prep, 1)
            dve.wait_ge(prep, 8 * p + 1)
            V.tensor_tensor(t1[:], t2[:], t1[:], ALU.subtract).then_inc(prep, 1)

        gla_gate(0)
        dve.wait_ge(sem("row_act"), 2)
        link(V.tensor_tensor(rows[:, 2, :], rows[:, 2, :], rows[:, 1, :], ALU.subtract))
        link(V.tensor_tensor_scan(rows[:, 1, :], rows[:, 2, :], rows[:, 2, :], 0.0, ALU.add, ALU.min))
        link(V.tensor_tensor(rows[:, 0, :], rows[:, 0, :], rows[:, 1, :], ALU.subtract))
        link(V.tensor_tensor_scan(rows[:, 3, :], rows[:, 0, :], rows[:, 0, :], 0.0, ALU.max, ALU.max))
        V.tensor_scalar(neg_g[:], rows[:, 3, :], -1.0, None, ALU.mult)
        V.tensor_tensor(rows[:, 2, :], rows[:, 1, :], rows[:, 3, :], ALU.add).then_inc(sem("row_step"), 1)

        dve.wait_ge(sem("in_mcon"), 32)
        for p in range(2):
            a0, d0 = 6 * p, 8 * p
            if p:
                gla_gate(1)
            dve.wait_ge(sem("prep_act"), a0 + 2)
            dve.wait_ge(prep, d0 + 2)
            V.tensor_tensor(t2[:], t2[:], t1[:], ALU.subtract).then_inc(prep, 1)
            dve.wait_ge(prep, d0 + 3)
            V.tensor_tensor_scan(scan_b[:], mcon[:, M_RESET:M_RESET + S], t2[:], 0.0, ALU.mult, ALU.add).then_inc(prep, 1)
            dve.wait_ge(sem("prep_act"), a0 + 3)
            wait_full(dve, "qa", p)
            V.scalar_tensor_tensor(q_in[:, p, :], ps[:, pair("qa") + p, :], 0.125, t1[:], ALU.mult, ALU.mult).then_inc(prep, 1)
            b3 = scan_b[:].rearrange("q (c t) -> q c t", t=CHUNK)
            V.tensor_tensor(t2[:].rearrange("q (c t) -> q c t", t=CHUNK),
                            b3[:, :, CHUNK - 1:CHUNK].to_broadcast([P, NCH, CHUNK]), b3, ALU.subtract).then_inc(prep, 1)
            dve.wait_ge(sem("prep_act"), a0 + 5)
            wait_full(dve, "ka", p)
            V.tensor_tensor(k_in[:, p, :], ps[:, pair("ka") + p, :], t1[:], ALU.mult).then_inc(prep, 1)
            dve.wait_ge(sem("prep_act"), a0 + 6)
            V.tensor_tensor(tmp[:, p, :], ps[:, pair("ka") + p, :], t2[:], ALU.mult).then_inc(prep, 1)
        dve.wait_ge(sem("am_full"), 1)
        V.tensor_copy(a_col, ps[:, 6, 0:16]).then_inc(sem("am_copied"), 1)

        def v_blocks(name):
            for tb in (1, 3):
                part = name if tb == 1 else name + "+"
                wait_full(dve, part, 1)
                V.tensor_copy(v_dst[name](tb), v_src(name, tb)).then_inc(sem("v_dve"), 1)

        v_blocks("va")

        def conv(p):
            for b in range(2):
                ch = 2 * p + b
                dve.wait_ge(sem("conv_in"), ch + 1)
                if ch >= 2:
                    dve.wait_ge(sem("qk_ready"), ch - 1)
                else:
                    dve.wait_ge(sem("kd_full"), 2)
                y = tmp[:, b, :]
                tap = lambda k: vcol(V_CW + k * KC + ch)
                link(V.tensor_scalar(y, q_raw[:, b, 3:3 + S], tap(3), vcol(V_CB + ch), ALU.mult, ALU.add))
                for k in (2, 1):
                    link(V.scalar_tensor_tensor(y, q_raw[:, b, k:k + S], tap(k), y, ALU.mult, ALU.add))
                V.scalar_tensor_tensor(y, q_raw[:, b, 0:S], tap(0), y, ALU.mult, ALU.add).then_inc(sem("conv_done"), 1)

        conv(0)
        dve.wait_ge(sem("prep_act"), 12)
        link(V.memset(gla_p[:], 0.0))
        for h in range(4):
            dve.wait_ge(sem("gla_s_full"), h + 1)
            V.copy_predicated(gla_p[:, h, :].rearrange("q (t d) -> q t d", t=TB),
                              mcon[:, M_SAME:M_SAME + P].bitcast(U32).unsqueeze(1).to_broadcast([P, TB, P]),
                              ps[:, GLA_BANK[h], :].rearrange("q (t d) -> q t d", t=TB)).then_inc(sem("gla_p_ready"), 1)
        conv(1)

        def states(p):
            for c in range(NCH - 1):
                dve.wait_ge(sem("kv_full"), 2 * p + (1 if c < 4 else 2))
                if c:
                    dve.wait_ge(sem("st_ready"), 7 * p + c)
                for e in range(2):
                    r = slice(64 * e, 64 * e + 64)
                    kv = ps[r, KV_BANK[c], (c // 2 % 2) * 256 + e * P:(c // 2 % 2) * 256 + (e + 1) * P]
                    if c == 0:
                        i = V.tensor_copy(st[r, p, 0, :], kv)
                    else:
                        i = V.scalar_tensor_tensor(st[r, p, c, :], st[r, p, c - 1, :], dec[r, p, c:c + 1], kv, ALU.mult, ALU.add)
                i.then_inc(sem("st_ready"), 1)

        dve.wait_ge(sem("am_full"), 1)
        states(0)
        ada_block(2)
        conv(2)
        states(1)
        conv(3)
        ada_block(3)
        v_blocks("vb")
        ada_block(4)

        for tb in range(TB):
            dve.wait_ge(sem("o_full"), tb + 1)
            if tb == 0:
                dve.wait_ge(sem("ra_ready"), TB)
            for h in range(4):
                i = V.bn_stats(stats[:, 4 * tb + h, :], ps[:, GLA_BANK[tb], tile_of(h)])
            link(i)
            for h in range(4):
                i = V.bn_aggr(mv[:, 4 * tb + h, :], stats[:, 4 * tb + h, :])
            link(i)
            for h in range(4):
                i = V.scalar_tensor_tensor(og[:, tb, tile_of(h)], ps[:, GLA_BANK[tb], tile_of(h)], mv[:, 4 * tb + h, 0:1],
                                           og[:, tb, tile_of(h)], ALU.subtract, ALU.mult)
            i.then_inc(sem("o_done"), 1)
        dve.wait_ge(sem("std_gla"), 1)
        link(V.reciprocal(rstd[:], cols[:, 5, :]))
        dve.wait_ge(sem("o_done"), TB)
        V.tensor_tensor(og[:, :, 0:S].rearrange("q t (h d) -> q t h d", h=4), og[:, :, 0:S].rearrange("q t (h d) -> q t h d", h=4),
                        rstd[:].rearrange("q (t h) -> q t h", t=TB).unsqueeze(3).to_broadcast([P, TB, 4, P]),
                        ALU.mult).then_inc(sem("og_ready"), 1)
        dve.wait_ge(sem("o_full"), TB)
        V.memset(cols[:, 2, 0:1], 0.0).then_inc(sem("pv_free"), 1)
        ada_block(5)

        def masked(h):
            dve.wait_ge(sem("ng_full"), h + 1)
            if h == 0:
                dve.wait_ge(sem("qk_ready"), KC)
            V.tensor_tensor(tmp[:, h % 2, :].rearrange("q (t d) -> q t d", t=TB),
                            ps[:, NG_BANK[h % 2], :].rearrange("q (t d) -> q t d", t=TB),
                            mcon[:, M_CAUSAL:M_CAUSAL + P].unsqueeze(1).to_broadcast([P, TB, P]),
                            ALU.add).then_inc(sem("ed_ready"), 1)

        def weigh(h):
            dve.wait_ge(sem("ml_w_ready"), h + 1)
            dve.wait_ge(sem("ml_s_full"), h + 1)
            if h >= 2:
                dve.wait_ge(sem("num_full"), h - 1)
            V.scalar_tensor_tensor(ml_a[:, h % 2, :], psf[:, 0:SC], P ** -0.5, ml_w[:, h % 2, :], ALU.mult, ALU.mult
                                   ).then_inc(sem("ml_a_ready"), 1)

        def ml_stats(h):
            dve.wait_ge(sem("num_ready"), h + 1)
            for tb in range(TB):
                V.bn_stats(stats2[:, 4 * h + tb, :], num[:, h, tb, 0:P])

        masked(0)
        masked(1)
        weigh(0)
        weigh(1)
        for h in range(4):
            if h + 2 < 4:
                dve.wait_ge(sem("ml_w_ready"), h + 1)
                masked(h + 2)
            ml_stats(h)
            if h + 2 < 4:
                weigh(h + 2)
        dve.wait_ge(sem("den_abs"), 1)
        dve.wait_ge(sem("em_ready"), 1)
        link(V.tensor_tensor(cols[:, 3, :].rearrange("q (h t) -> q h t", h=4), cols[:, 2, :].rearrange("q (h t) -> q h t", h=4),
                             em_col.rearrange("q (t h) -> q h t", h=4), ALU.max))
        for i in range(16):
            ins = V.bn_aggr(mv2[:, i, :], stats2[:, i, :])
        link(V.reciprocal(cols[:, 3, :], cols[:, 3, :]))
        link(V.tensor_tensor(cols[:, 4, :], mv2[:, :, 1], cols[:, 3, :], ALU.mult))
        V.tensor_tensor(cols[:, 4, :], cols[:, 4, :], cols[:, 3, :], ALU.mult).then_inc(sem("ml_var"), 1)
        dve.wait_ge(sem("ob_ready"), TB)
        for h in range(4):
            for tb in range(TB):
                o = og[:, tb, S + h * P:S + (h + 1) * P]
                i = V.scalar_tensor_tensor(o, num[:, h, tb, 0:P], mv2[:, 4 * h + tb, 0:1], o, ALU.subtract, ALU.mult)
        link(i)
        dve.wait_ge(sem("ml_std"), 1)
        link(V.reciprocal(rstd[:], cols[:, 4, :]))
        link(V.tensor_tensor(rstd[:], rstd[:], cols[:, 3, :], ALU.mult))
        o4 = og[:, :, S:D].rearrange("q t (h d) -> q h t d", h=4)
        V.tensor_tensor(o4, o4, rstd[:].rearrange("q (h t) -> q h t", h=4).unsqueeze(3).to_broadcast([P, 4, TB, P]),
                        ALU.mult).then_inc(sem("og_ready"), 1)
        for n in range(KC):
            e = H_BASE["cat0"] + n
            dve.wait_ge(sem("cat_full"), n + 1)
            tmp_free(e)
            V.tensor_scalar(tmp[:, e % 2, :], ps[:, 4 + n % 2, :], vcol(V_GN + n), None, ALU.mult).then_inc(sem("h_tmp_ready"), 1)
            if n >= 1:
                lo_of_chunk(e - 1, n - 1)
        lo_of_chunk(H_BASE["cat0"] + KC - 1, KC - 1)

        def norm(i, names, rt, extra=None):
            V.tensor_scalar(gate1[:, i, :], mod[:, (2, 5, 8, 11)[i], :], 1.0, None, ALU.add)
            if i < 3:
                derive(i + 1, (3, 6, 9)[i], (4, 7, 10)[i], i)
            else:
                link(V.tensor_scalar(mx0[:, 0:1], zero_col, 1.0, None, ALU.mult))
            dve.wait_ge(sem("xa_ready"), KC * (i + 1))

            def half_stats(half):
                dve.wait_ge(sem("rt_ready"), KC * i + 4 * half + 4)
                for tb in range(TB):
                    ins = V.bn_stats(stats[:, 2 * tb + half, :], rt[:, tb, half * S:(half + 1) * S])
                return ins

            for n in range(KC):
                wait_full(dve, names[n // 2], n % 2)
                V.scalar_tensor_tensor(xa[:, n, :], ps[:, pair(names[n // 2]) + n % 2, :], gate1[:, i, n:n + 1], xa[:, n, :],
                                       ALU.mult, ALU.add).then_inc(sem("r_ready"), 1)
                if n == 1 and extra:
                    extra()
                if n == 5:
                    half_stats(0)
            link(half_stats(1))
            for tb in range(TB):
                ins = V.bn_aggr(mv[:, tb, :], stats[:, 2 * tb:2 * tb + 2, :].rearrange("p a b -> p (a b)"))
            ins.then_inc(sem("mv_ready"), 1)
            dve.wait_ge(sem("std_ready"), i + 1)
            link(V.reciprocal(rstd[:, 0:TB], cols[:, 5, 0:TB]))
            for tb in range(TB):
                V.tensor_scalar(xh[:, tb, :], rt[:, tb, :], mv[:, tb, 0:1], rstd[:, tb:tb + 1], ALU.subtract, ALU.mult
                                ).then_inc(sem("xh_ready"), 1)
            if i == 3:
                dve.wait_ge(sem("in_rows"), 16)
                for tb in range(TB):
                    dve.wait_ge(sem("xh_ready"), TB * i + tb + 1)
                    link(V.tensor_tensor(xh[:, tb, :], xh[:, tb, :], rows_gb[:, 0, :], ALU.mult))
                    V.tensor_tensor(xh[:, tb, :], xh[:, tb, :], rows_gb[:, 1, :], ALU.add).then_inc(sem("out_ready"), 1)
                return
            base = H_BASE[f"norm{i}"]
            for n in range(KC):
                name = f"norm{i}_{n // 2}"
                wait_full(dve, name, n % 2)
                chunk_from(base + n, n, ps[:, pair(name) + n % 2, :], i + 1)
                if n >= 1:
                    lo_of_chunk(base + n - 1, n - 1)
            lo_of_chunk(base + KC - 1, KC - 1)

        def ffn(layer):
            s0 = STAGES[f"ffn{layer}"][0]
            f0 = uses[where[f"up{layer}_0"]][1][0][1]
            up = pair(f"up{layer}_0")

            def step(j, first=False):
                for b in range(2):
                    dve.wait_ge(*((sem("bank_full"), 2 * j + f0) if b == 0 else (sem("slot_done"), 4 * j + (s0 + 4))))
                    dve.wait_ge(sem("silu_ready"), 2 * j + (FC * layer + 1 + b))
                    V.tensor_tensor(tmp[:, b, :], tmp[:, b, :], ps[:, up + b, :], ALU.mult).then_inc(sem("prod_ready"), 1)
                for b in range(2):
                    dve.wait_ge(sem("hid_hi_ready"), 2 * j + (FC * layer + 1 + b))
                    at_ = (lambda t: t[:, b, :]) if first else (lambda t: t[:, bass.ds(2 * j + b, 1), :].rearrange("p o t -> p (o t)"))
                    V.tensor_tensor(at_(hid_lo), tmp[:, b, :], at_(hid_hi).bitcast(F32), ALU.subtract).then_inc(sem("hid_ready"), 1)

            step(0, True)
            if layer == 1:
                with dve.Fori(1, FC // 2) as j:
                    step(j)
                return
            with dve.Fori(0, FC // 4) as it:
                dve.wait_ge(sem("ada_cols"), it + 6)
                V.tensor_tensor(mod[:, bass.ds(it + 5, 1), :].rearrange("p o t -> p (o t)"), ps[:, 7, 0:KC],
                                vec[:, bass.ds(KC * it + (V_ADAB + 5 * KC), KC)], ALU.add).then_inc(sem("mod_ready"), 1)
                for u in range(2):
                    for k in range(4 * u, 4 * u + 4):
                        dve.wait_ge(sem(f"ada_landed{k % 2}"), 64 * it + 16 * (16 + k // 2 + 1))
                        if k:
                            dve.wait_ge(sem("ada_step"), 8 * it + (48 + k))
                            V.scalar_tensor_tensor(ada_acc[:], ada_raw[:, k % 2, :], c_act[:, k:k + 1], ada_acc[:], ALU.mult,
                                                   ALU.add).then_inc(sem("ada_step"), 1)
                        else:
                            V.tensor_scalar(ada_acc[:], ada_raw[:, 0, :], c_act[:, 0:1], None, ALU.mult
                                            ).then_inc(sem("ada_step"), 1)
                    step(2 * it + (u + 1))

        norm(0, [f"out0{p}" for p in range(4)], rt_mixer)
        ffn(0)
        norm(1, [f"down0{p}" for p in range(4)], rt_ffn, lambda: ada_block(11))
        mod_block(11)

        for name, dst, panels, scale in (("qc", qc, 2, 0.125), ("kc", kc, 2, 1.0), ("qd", qd, 3, 0.125), ("kd", kd, 3, 1.0)):
            for p in range(panels):
                part = f"{name}{p}"
                wait_full(dve, part, 1)
                V.tensor_scalar(dst[:, 2 * p + 1, :], ps[:, pair(part) + 1, :], scale, None, ALU.mult).then_inc(sem("qk1_dve"), 1)
            if name == "qc":
                dve.wait_ge(sem("f_full"), 1)
                for g in range(3):
                    V.tensor_copy(f_rows[:, g, 0:S], ps[0:4, (4, 6, 7)[g], :])
                V.tensor_copy(f_rows[:, :, S:F_LEN], ps[0:4, 5, 0:3 * P].rearrange("q (g x) -> q g x", g=3)
                              ).then_inc(sem("f_ready"), 1)
        for name in ("vc", "vd0", "vd1"):
            v_blocks(name)

        def diag_tiles(t):
            return (t[:, 0:2 * S].rearrange("q (a x) -> q a x", a=2)[:, :, 0:P], t[:, OFS[3]:OFS[3] + 2 * P].rearrange("q (a x) -> q a x", a=2))

        def twice(ap):
            return ap.unsqueeze(1).to_broadcast([P, 2, P])

        def softplus(h):
            dve.wait_ge(sem("sb_act"), 3 * h + 3)
            if h >= 2:
                dve.wait_ge(sem("tri_full"), h - 1)
            if h == 0:
                dve.wait_ge(sem("f_stored"), 16)
            sp_ = sb_sp[h % 2]
            link(V.scalar_tensor_tensor(sp_[:], psf[:, SB_COL[h % 2]:SB_COL[h % 2] + SC], 0.0, sb_a[h % 2][:], ALU.max, ALU.add))
            for t in diag_tiles(sp_):
                i = V.tensor_tensor(t, t, twice(cst[:, C_KEEP:C_KEEP + P]), ALU.mult)
            i.then_inc(sem("sp_ready"), 1)

        def att_mask(h):
            dve.wait_ge(sem("att_exp"), h + 1)
            for t in diag_tiles(sb_a[h % 2]):
                i = V.copy_predicated(t, twice(cst[:, C_DROP:C_DROP + P]).bitcast(U32), zero_col.unsqueeze(1).to_broadcast([P, 2, P]))
            i.then_inc(sem("att_ready"), 1)

        def sb_chunk(n):
            e = H_BASE["cat1"] + n
            dve.wait_ge(sem("av_done"), 2 * n + 2)
            tmp_free(e)
            V.tensor_copy(tmp[:, e % 2, :], ps[:, 6 + n % 2, :]).then_inc(sem("h_tmp_ready"), 1)
            lo_of_chunk(e, n)

        softplus(0)
        for h in range(8):
            if h + 1 < 8:
                softplus(h + 1)
            att_mask(h)
            if h % 2 == 0 and h >= 2:
                sb_chunk(h // 2 - 1)
        sb_chunk(3)

        def dil_logits(i):
            h, t = divmod(i, TB)
            w = (t + 1) * P
            w0 = min(2, t + 1) * P
            if t == 0:
                dve.wait_ge(sem(f"strip{h}"), 48)
            if i >= 2:
                dve.wait_ge(sem("turn_ready"), rounds(i - 2)[-1][0] + 1)
            dve.wait_ge(sem("l_full"), i + 1)
            base = 3 * (i % 2)
            dst = lg[i % 2]
            for b in range(2):
                V.tensor_tensor(dst[:, b * w:(b + 1) * w], ps[:, base + b, 0:w], strip[h][:, (b + 1) * S - w:(b + 1) * S], ALU.add)
            link(V.tensor_tensor(dst[:, 2 * w:2 * w + w0], ps[:, base + 2, 0:w0], strip[h][:, SC - w0:SC], ALU.add))
            link(V.tensor_reduce(mx0[:, i:i + 1], dst[:, 0:2 * w + w0], mybir.AxisListType.X, ALU.max))
            V.tensor_scalar(mx1[:, i:i + 1], mx0[:, i:i + 1], -1.0, None, ALU.mult).then_inc(sem("dil_max"), 1)

        dil_logits(0)
        for i in range(4 * TB):
            if i + 1 < 4 * TB:
                dil_logits(i + 1)
            h, t = divmod(i, TB)
            if t == TB - 1:
                dve.wait_ge(sem("pv_done"), i + 1)
                dve.wait_ge(sem("dil_p"), i + 1)
                link(V.reciprocal(rstd[:, 4 * h:4 * h + 4], den[:, 4 * h:4 * h + 4]))
                V.tensor_tensor(od[:, :, h * 64:h * 64 + 64], ps[:, 7, 0:256].rearrange("q (t d) -> q t d", t=TB),
                                rstd[:, 4 * h:4 * h + 4].unsqueeze(2).to_broadcast([P, TB, 64]), ALU.mult).then_inc(sem("od_ready"), 1)
        for n in range(4, 6):
            e = H_BASE["cat1"] + n
            dve.wait_ge(sem("cat_full"), KC + n - 3)
            tmp_free(e)
            V.tensor_copy(tmp[:, e % 2, :], ps[:, n, :]).then_inc(sem("h_tmp_ready"), 1)
            lo_of_chunk(e, n)
        norm(2, [f"out1{p}" for p in range(4)], rt_mixer)
        ffn(1)
        norm(3, [f"down1{p}" for p in range(4)], rt_ffn)

    ctx.close()


def weight_stream(w):
    s = np.zeros((N_SLOTS, P, SLOT), np.float32)

    def tiles(a, k, n):
        return a.reshape(k, P, n).transpose(1, 0, 2).reshape(P, k * n)

    def panel(name, a, nk):
        first = STAGES[name][0]
        for i, (k0, n) in enumerate(panel_slots(nk)):
            s[first + i, :, :n * 256] = tiles(a[k0 * P:(k0 + n) * P], n, 256)

    def group(name, a, kk, width):
        first, count = STAGES[name]
        for i in range(count):
            s[first + i] = tiles(a[i * kk * P:(i + 1) * kk * P], kk, width)

    ab, cd = w["ab_w_in"][0], w["cd_w_in"][0]
    narrow = np.zeros((D, P), np.float32)
    narrow[:, 0:16] = ab[:, 1536:1552]
    narrow[:, 32:36] = ab[:, 3088:3092]
    narrow[:, 64:68] = ab[:, 3092:3096]
    s[0] = tiles(narrow, KC, P)
    panel("qa", ab[:, 0:256], KC)
    panel("ka", ab[:, 256:512], KC)
    group("va", ab[:, 512:1024], 2, S)
    for p in range(4):
        panel(f"qkb{p}", ab[:, 1552 + 256 * p:1808 + 256 * p], KC)
    group("vb", ab[:, 2576:3088], 2, S)
    group("ra", ab[:, 1024:1536], 2, S)
    group("ob", ab[:, 3096:3608], 2, S)
    for layer, wo, nk in ((0, w["ab_w_out"][0], KC), (1, w["cd_w_out"][0], 6)):
        for p in range(4):
            panel(f"out{layer}{p}", wo[:, 256 * p:256 * (p + 1)], nk)
            panel(f"down{layer}{p}", w["ffn_w2"][layer][:, 256 * p:256 * (p + 1)], FC)
        for j in range(FC // 2):
            first = STAGES[f"ffn{layer}"][0] + 4 * j
            for i, a in enumerate((w["ffn_w1"][layer], w["ffn_w3"][layer])):
                for half in range(2):
                    s[first + 2 * i + half] = tiles(a[512 * half:512 * (half + 1), 256 * j:256 * (j + 1)], 4, 256)
    col = 0
    for name, panels in (("qc", 2), ("kc", 2)):
        for p in range(panels):
            panel(f"{name}{p}", cd[:, col:col + 256], KC)
            col += 256
    group("vc", cd[:, col:col + 512], 2, S)
    col += 512
    for name, panels in (("qd", 3), ("kd", 3)):
        for p in range(panels):
            panel(f"{name}{p}", cd[:, col:col + 256], KC)
            col += 256
    group("vd0", cd[:, col:col + 512], 2, S)
    group("vd1", cd[:, col + 512:col + 768], 4, 256)
    return s


def kernel(**inputs):
    import concourse.bacc as bacc
    from concourse.bass_utils import run_bass_kernel_spmd

    w = {k: np.asarray(v) for k, v in inputs.items()}
    chunks = lambda a: a.reshape(-1, P).T
    vecs = np.zeros((P, V_N), np.float32)
    vecs[:, V_C:V_C + KC] = chunks(w["c"])
    vecs[:, V_ADAB:V_ADAB + 96] = chunks(w["ada_b"])
    vecs[:, V_LNG:V_LNG + 32] = chunks(w["ln_g"])
    vecs[:, V_LNB:V_LNB + 32] = chunks(w["ln_b"])
    vecs[:, V_BA:V_BA + 2] = chunks(w["gla_ba"])
    vecs[:, V_GN:V_GN + 4] = chunks(w["gla_norm_g"])
    vecs[:, V_GN + 4:V_GN + 8] = chunks(w["ml_norm_g"])
    vecs[:, V_CW:V_CW + 32] = chunks(w["ml_conv_w"])
    vecs[:, V_CB:V_CB + KC] = chunks(w["ml_conv_b"])
    vecs[32:36, V_BI] = w["ml_b_i"][0]
    vecs[64:68, V_BF] = w["ml_b_f"][0]
    const, const0 = constants()
    rel = np.ones((N_BUCKETS + 1, 12), np.float32)
    rel[0:N_BUCKETS] = w["rel_bias"]
    ada = w["ada_w"].reshape(2, KC, P, 6, D).transpose(0, 3, 1, 2, 4).reshape(12 * KC, P, D)
    arrays = {
        "wstream": weight_stream(w),
        "astream": np.ascontiguousarray(ada),
        "xT": np.ascontiguousarray(w["x"][0].T),
        "vecs": vecs,
        "const": const,
        "const0": const0,
        "wa_up": np.ascontiguousarray(w["gla_wa_up"][0]),
        "dsel": distance_select(),
        "rel": rel,
        "ln_rows": np.ascontiguousarray(np.broadcast_to(np.stack([w["ln_g"][1, 1], w["ln_b"][1, 1]]), (P, 2, D))),
    }
    nc = bacc.Bacc("TRN2", target_bir_lowering=False, num_devices=1)
    args = {n: nc.dram_tensor(n, a.shape, F32, kind="ExternalInput").ap() for n, a in arrays.items()}
    out = nc.dram_tensor("out", (S, D), F32, kind="ExternalOutput").ap()
    build_program(nc, **args, out=out)
    r = run_bass_kernel_spmd(nc, [arrays], core_ids=[0])
    return r.results[0]["out"].reshape(1, S, D)
```

```python
from contextlib import ExitStack

import numpy as np

import concourse.bass as bass
from concourse import mybir

ALU = mybir.AluOpType
ACT = mybir.ActivationFunctionType
F32 = mybir.dt.float32
F32R = mybir.dt.float32r
U32 = mybir.dt.uint32

P = 128
D = 1024
S = 512
KC = D // P
TB = S // P
D_FF = 2816
FC = D_FF // P
CHUNK = 64
NCH = S // CHUNK
ALPHA = 4 ** 0.25
EPS = 1e-5
TAU = 16.0
NEG = -1e30
SLOT = 1024
RAW = 4
RING = 4
CONV_RING = 6
DIL = ((128, 1), (512, 4), (2048, 16))
RES = 4
assert all(dil % RES == 0 and window // dil * RES >= P for window, dil in DIL[1:])
N_BUCKETS, REL_MAX = 32, 2048



def panel_slots(nk):
    return [(k, min(4, nk - k)) for k in range(0, nk, 4)]


def stage_table():
    table, n = {}, 0

    def add(name, count):
        nonlocal n
        table[name] = (n, count)
        n += count

    add("narrow", 1)
    add("va", 4)
    for name in ("qa", "ka"):
        add(name, 2)
    for p in range(4):
        add(f"qkb{p}", 2)
    for name in ("vb", "ra", "ob"):
        add(name, 4)
    for p in range(4):
        add(f"out0{p}", 2)
    for layer in (0, 1):
        if layer == 1:
            for name, panels in (("qc", 2), ("kc", 2), ("vc", 0), ("qd", 3), ("kd", 3)):
                for p in range(panels):
                    add(f"{name}{p}", 2)
                if name == "vc":
                    add("vc", 4)
            add("vd0", 4)
            add("vd1", 2)
            for p in range(4):
                add(f"out1{p}", 2)
        add(f"ffn{layer}", 4 * (FC // 2))
        for p in range(4):
            add(f"down{layer}{p}", len(panel_slots(FC)))
    return table, n


STAGES, N_SLOTS = stage_table()


def t5_bucket(dist):
    exact = N_BUCKETS // 2
    dd = np.maximum(dist, 1).astype(np.float64)
    large = exact + (np.log(dd / exact) / np.log(REL_MAX / exact) * (N_BUCKETS - exact)).astype(np.int32)
    return np.where(dist < exact, dist, np.minimum(large, N_BUCKETS - 1)).astype(np.int32)


F_LEN = 384
SKEW = F_LEN + P


def distance_select():
    sel = np.zeros((N_BUCKETS + 1, 3, F_LEN), np.float32)
    for g, (window, dil) in enumerate(DIL):
        for x in range(F_LEN):
            d = 2 * P - 1 - x if g == 0 else RES * (P - 1 - x)
            if 0 <= d <= window and d % dil == 0:
                sel[t5_bucket(np.array([d]))[0], g, x] = 1.0
            else:
                sel[N_BUCKETS, g, x] = NEG
    return sel


C_IDENT, C_ONE, C_ZERO, C_KEEP, C_DROP, C_TRI, C_ONES = 0, 128, 129, 130, 258, 386, 514
C_N = 642
M_RESET, M_SEL, M_SAME, M_CAUSAL, M_WAUP = 0, 512, 1024, 1152, 1280
M_N = 1536


def constants():
    c = np.zeros((P, C_N), np.float32)
    r = np.arange(P)
    c[:, C_IDENT:C_IDENT + P] = np.eye(P)
    c[:, C_ONE] = 1.0
    c[:, C_KEEP:C_KEEP + P] = r[:, None] < r[None, :]
    c[:, C_DROP:C_DROP + P] = r[:, None] >= r[None, :]
    c[:, C_TRI:C_TRI + P] = -(r[:, None] >= r[None, :]).astype(np.float32)
    c[:, C_ONES:C_ONES + P] = -1.0
    m = np.zeros((P, M_WAUP), np.float32)
    m[:, M_RESET:M_RESET + S] = (np.arange(S) % CHUNK != 0)[None, :]
    for h in range(4):
        m[h, M_SEL + h * P:M_SEL + (h + 1) * P] = 1.0
    m[:, M_SAME:M_SAME + P] = (r[:, None] // CHUNK == r[None, :] // CHUNK) & (r[:, None] <= r[None, :])
    m[:, M_CAUSAL:M_CAUSAL + P] = np.where(r[:, None] <= r[None, :], 0.0, NEG)
    return c, m


V_C = 0
V_ADAB = V_C + KC
V_LNG = V_ADAB + 96
V_LNB = V_LNG + 32
V_BA = V_LNB + 32
V_GN = V_BA + 2
V_CW = V_GN + KC
V_CB = V_CW + 32
V_BI = V_CB + KC
V_BF = V_BI + 1
V_N = V_BF + 1

OFS = (0, 512, 1024, 896)
WID = tuple(S - P * j for j in range(TB))
SC = 1280


def build_program(nc, wstream, astream, xT, vecs, const, const0, wa_up, dsel, rel, ln_rows, out):
    ctx = ExitStack()
    sems = {}

    def sem(name):
        if name not in sems:
            sems[name] = ctx.enter_context(nc.semaphore(name))
        return sems[name]

    place = [16512]

    def at(name, shape, dt=F32, offset=None):
        size = int(np.prod(shape[1:])) * 4
        size = (size + 31) // 32 * 32
        if offset is None:
            offset = place[0]
            place[0] += size
        return nc.alloc_sbuf_tensor_at(name, shape, dt, offset=offset)

    xa = at("xa", [P, KC, S])
    hi_at = place[0]
    h_hi = at("h_hi", [P, KC, S], F32R)
    h_lo = at("h_lo", [P, KC, S], F32R)
    raw = at("raw", [P, RAW, SLOT])
    w_hi = at("w_hi", [P, RING, SLOT], F32R)
    w_lo = at("w_lo", [P, RING, SLOT], F32R)
    ada_raw_at = place[0]
    ada_raw = at("ada_raw", [P, 2, SLOT])
    ada_acc = at("ada_acc", [P, SLOT])
    tmp = at("tmp", [P, 2, S])
    cst = at("cst", [P, C_N])
    vec = at("vec", [P, V_N])
    c_act = at("c_act", [P, KC])
    mod = at("mod", [P, 12, KC])
    scl = at("scl", [P, 4, KC])
    bia = at("bia", [P, 4, KC])
    gate1 = at("gate1", [P, 4, KC])
    lnga = at("lnga", [P, 4, KC])
    lnba = at("lnba", [P, 4, KC])
    stats = at("stats", [P, 16, 6])
    mv = at("mv", [P, 16, 2])
    rstd = at("rstd", [P, 16])
    stats2 = at("stats2", [P, 16, 6])
    mv2 = at("mv2", [P, 16, 2])
    cols = at("cols", [P, 6, 16])
    vec_eps = at("vec_eps", [P, 1])
    nmr = at("nmr", [P, TB])
    warm = at("warm", [P, 1])
    arena = place[0]
    assert arena + 22528 * 4 <= 229344, arena

    def ar(name, shape, col, dt=F32):
        assert arena + (col + int(np.prod(shape[1:]))) * 4 <= 229344, (name, arena)
        return at(name, shape, dt, offset=arena + 4 * col)

    hid_hi = ar("hid_hi", [P, FC, S], 0, F32R)
    hid_lo = ar("hid_lo", [P, FC, S], FC * S, F32R)
    xh = ar("xh", [P, TB, D], 0)
    rt_mixer = ar("rt_mixer", [P, TB, D], 4096)
    rt_ffn = at("rt_ffn", [P, TB, D], offset=hi_at)
    ada_first = ar("ada_first", [P, 16, SLOT], 0)
    x_in = ar("x_in", [P, KC, S], 16384)
    rows_gb = at("rows_gb", [P, 2, D], offset=hi_at + KC * S * 4)
    og = ar("og", [P, TB, D], 0)
    va = ar("va", [P, TB, S], 4096)
    vb = ar("vb", [P, TB, 4, 129], 6144)
    qk = ar("qk", [P, KC, S], 8208)
    q_in = ar("q_in", [P, 2, S], 12304)
    k_in = ar("k_in", [P, 2, S], 13328)
    kdt = ar("kdt", [P, TB, 2, P], 14352)
    st = ar("st", [P, 2, 8, P], 15376)
    rows = ar("rows", [4, 4, S], 15376)
    ml_w = ar("ml_w", [P, 2, SC], 12304)
    ml_a = ar("ml_a", [P, 2, SC], 14864)
    t1, t2, t3, scan_b = (ar(n, [P, 2, S], 1024 * i) for i, n in enumerate(("gate_t1", "gate_t2", "gate_t3", "scan_b")))
    a_low = ar("a_low", [16, S], 18960)
    gla_p = ar("gla_p", [P, 4, S], 17424)
    num = ar("num", [P, 4, TB, 129], 17424)
    neg_g = ar("neg_g", [4, S], 19488)
    q_raw = ar("q_raw", [P, CONV_RING, S + 3], 0)
    dec = ar("dec", [P, 2, NCH], 21040)
    mcon = ar("mcon", [P, M_N], 23008 - M_N)
    a_col, em_col = cols[:, 0, :], cols[:, 1, :]
    qc = ar("qc", [P, 4, S], 0)
    kc = ar("kc", [P, 4, S], 2048)
    vc = ar("vc", [P, TB, S], 4096)
    qd = ar("qd", [P, 6, S], 6144)
    kd = ar("kd", [P, 6, S], 9216)
    vd = ar("vd", [P, TB, 6, 3, 64], 12288)
    sb_a = [ar(f"sb_a{i}", [P, SC], 16896 + 2560 * i) for i in range(2)]
    sb_sp = [ar(f"sb_sp{i}", [P, SC], 18176 + 2560 * i) for i in range(2)]
    bt = at("bt", [P, 4, 512], offset=ada_raw_at)
    sel_sb = ar("sel_sb", [33, 3, F_LEN], 16896)
    rel_sb = ar("rel_sb", [33, 12], 18080)
    f_rows = ar("f_rows", [4, 3, F_LEN], 19456)
    f_dram = nc.dram_tensor("f_scratch", (12, F_LEN), F32, kind="Internal").ap()
    skew = nc.dram_tensor("skew_scratch", (12, P, SKEW), F32, kind="Internal").ap()
    lgs = (ar("lg_dil", [P, 4, TB, 256], 0), ar("lg_loc", [P, 4, TB, 256], 16896))
    pt = ar("pt", [P, 4, S], 4096)
    m_rows = ar("m_rows", [4, S], 20992)
    rec = ar("rec", [P, S], 21504)
    mx = cols[:, 2:4, :]
    nm = cols[:, 0:2, :]

    ps = ctx.enter_context(nc.psum_tensor("ps", [P, 8, S], F32))
    psf = ps[:].rearrange("p b n -> p (b n)")
    ident = cst[:, C_IDENT:C_IDENT + P]
    one_col = cst[:, C_ONE:C_ONE + 1]
    zero_col = cst[:, C_ZERO:C_ZERO + 1]

    full_count = [0]
    uses = []
    where = {}

    def use(name, free, last_slot=None, own=1):
        i = len(uses)
        full = []
        for b in range(2):
            if b < own or last_slot is None:
                full_count[0] += 1
                full.append(("bank_full", full_count[0]))
            else:
                full.append(("slot_done", last_slot + 1))
        uses.append((i % 2, full, free))
        where[name] = i

    def last(name):
        first, n = STAGES[name]
        return first + n - 1

    use("narrow", [("low_ready", 1), ("row_step", 3)], 0)
    V_FREE = {"va": 0, "vb": 1, "vc": 2, "vd0": 3, "vd1": 4}

    def group(name, free0, free1):
        use(name, free0, last(name), own=2)
        use(name + "+", free1, last(name))

    def vgroup(name):
        i = V_FREE[name]
        group(name, [("v_act", 2 * i + 1), ("v_dve", 2 * i + 1)], [("v_act", 2 * i + 2), ("v_dve", 2 * i + 2)])

    vgroup("va")
    use("qa", [("prep_dve", 12)], last("qa"))
    use("ka", [("prep_dve", 16)], last("ka"))
    for p in range(4):
        use(f"qkb{p}", [("conv_in", 2 * p + 2)], last(f"qkb{p}"))
    vgroup("vb")
    group("ra", [("ra_ready", 2)], [("ra_ready", 4)])
    group("ob", [("ob_ready", 2)], [("ob_ready", 4)])
    for norm in range(4):
        layer = norm // 2
        if norm % 2 == 0:
            if layer == 1:
                for i, (name, panels) in enumerate((("qc", 2), ("kc", 2), ("qd", 3), ("kd", 3))):
                    base = (0, 2, 4, 7)[i]
                    for p in range(panels):
                        e = base + p
                        use(f"{name}{p}", [("qk1_act", e + 1), ("qk1_dve", e + 1)], last(f"{name}{p}"))
                    if name == "kc":
                        vgroup("vc")
                vgroup("vd0")
                vgroup("vd1")
            down = [f"out{layer}{p}" for p in range(4)]
        else:
            for j in range(FC // 2):
                use(f"gate{layer}_{j}", [("silu_ready", FC * layer + 2 * j + 2)], STAGES[f"ffn{layer}"][0] + 4 * j + 1)
                use(f"up{layer}_{j}", [("prod_ready", FC * layer + 2 * j + 2)], STAGES[f"ffn{layer}"][0] + 4 * j + 3)
            down = [f"down{layer}{p}" for p in range(4)]
        for p, name in enumerate(down):
            use(name, [("r_ready", KC * norm + 2 * p + 2)], last(name))
        if norm < 3:
            for p in range(4):
                use(f"norm{norm}_{p}", [("xa_ready", KC * (norm + 1) + 2 * p + 2)])

    def pair(name):
        return 2 * uses[where[name]][0]

    def wait_full(eng, name, b):
        s, v = uses[where[name]][1][b]
        eng.wait_ge(sem(s), v)

    def wait_pair(eng, name):
        i = where[name]
        if i >= 2:
            for s, v in uses[i - 2][2]:
                eng.wait_ge(sem(s), v)

    def wait_free(eng, name):
        for s, v in uses[where[name]][2]:
            eng.wait_ge(sem(s), v)

    H_BASE = {"in": 0, "cat0": 8, "norm0": 16, "norm1": 24, "cat1": 32, "norm2": 38}



    def tile_of(n, width=P):
        return slice(n * width, (n + 1) * width)


    eps_col = vec_eps[:]
    GLA_BANK = (4, 5, 6, 7)
    O_BANK = (4, 5, 6, 4)
    KV_BANK = (4, 5, 4, 5, 6, 7, 6)
    NG_BANK = (3, 6)
    AV_BANK = (7, 7, 7, 3)

    def sb_col(h):
        return 0 if h > 4 and h % 2 else 4 * S

    FILL = [f"qd{p}" for p in range(3)] + [f"kd{p}" for p in range(3)] + ["vd0", "vd1"]

    v_dst = {
        "va": lambda tb: va[:, tb, :],
        "vb": lambda tb: vb[:, tb, :, 0:P],
        "vc": lambda tb: vc[:, tb, :],
        "vd0": lambda tb: vd[:, tb, 0:4, 0:3:2, :],
        "vd1": lambda tb: vd[:, tb, 4:6, 0:3:2, :],
    }

    def v_src(name, tb):
        part, b = (name, tb) if tb < 2 else (name + "+", tb - 2)
        bank = ps[:, pair(part) + b, :]
        if name == "vb":
            return bank.rearrange("q (h d) -> q h d", h=4)
        if name[:2] == "vd":
            return (bank[:, 0:256] if name == "vd1" else bank).rearrange("q (a b d) -> q a b d", b=2, d=64)
        return bank

    def by_residue(ap):
        return ap.rearrange("q (p t) -> q t p", t=RES)

    def score_step(s):
        return 2 * (s // 8) + s % 2, s % 8 // 2

    def score_bank(s):
        h, part = score_step(s)
        return (0, 1, 2, 4)[2 * (part % 2) + h % 2]

    def part_tiles(part):
        return range(1 if part == 3 else 0, TB)

    def lg_tiles(h, part):
        c = (0, P, P, 0)[part]
        return lgs[part // 2][:, h, part_tiles(part)[0]:TB, c:c + P]

    def bt_tile(h, part):
        c = (0, P, 3 * P, 2 * P)[part]
        return bt[:, h, c:c + P]

    def skew_rows(eng):
        eng.dma_start(bass.AP(skew.tensor, 0, [[P * SKEW, 12], [SKEW + 1, P], [1, F_LEN]]),
                      bass.AP(f_dram.tensor, 0, [[F_LEN, 12], [0, P], [1, F_LEN]])).then_inc(sem("skewed"), 16)

    def load_bias(eng):
        for col, g, n in ((0, 1, P), (P, 2, P), (2 * P, 0, 2 * P)):
            eng.dma_start(bt[:, :, col:col + n], skew.rearrange("(h g) q x -> g q h x", g=3)[g][:, :, P - 1:P - 1 + n]
                          ).then_inc(sem("bt_loaded"), 16)

    def turn_out(pe, i, p):
        for n in (2 * p, 2 * p + 1):
            pe.wait_ge(sem("r_ready"), KC * i + n + 1)
            if n >= 2:
                pe.wait_ge(sem("rt_ready"), KC * i + n - 1)
            for tb in range(TB):
                m = pe.transpose(ps[:, 4 + n % 2, tile_of(tb)], xa[:, n, tile_of(tb)], ident)
            m.then_inc(sem("rt_full"), 1)

    block = ctx.enter_context(nc.Block())

    ADA_AFTER = {5: 2, 23: 3, 34: 4}

    @block.sync
    def _(sp):
        sp.dma_start(vec[:], vecs).then_inc(sem("in_vec"), 16)
        for q in range(4):
            sp.dma_start(ada_first[:, 4 * q:4 * q + 4, :],
                         astream[4 * q:4 * q + 4].rearrange("s p n -> p s n")).then_inc(sem(f"in_ada{q}"), 16)
            if q == 1:
                sp.dma_start(cst[:], const).then_inc(sem("in_const"), 16)
            if q == 3:
                sp.dma_start(x_in[:, 0:4, :], xT[0:4 * P].rearrange("(k p) t -> p k t", p=P)).then_inc(sem("in_x0"), 16)
        sp.dma_start(raw[:, 0, :], wstream[0]).then_inc(sem("raw_landed0"), 16)
        sp.dma_start(x_in[:, 4:8, :], xT[4 * P:].rearrange("(k p) t -> p k t", p=P)).then_inc(sem("in_x1"), 16)
        for s in range(1, RAW):
            sp.dma_start(raw[:, s, :], wstream[s]).then_inc(sem(f"raw_landed{s}"), 16)
        sp.dma_start(mcon[:, 0:M_WAUP], const0).then_inc(sem("in_mcon"), 16)
        sp.dma_start(mcon[0:16, M_WAUP:M_N], wa_up).then_inc(sem("in_mcon"), 16)

        def load(s):
            if s >= RAW:
                sp.wait_ge(sem("w_lo_ready"), s - RAW + 1)
            sp.dma_start(raw[:, s % RAW, :], wstream[s]).then_inc(sem(f"raw_landed{s % RAW}"), 16)

        def load_ada(i):
            if i >= 18:
                sp.wait_ge(sem("ada_step"), i - 1)
            sp.dma_start(ada_raw[:, i % 2, :], astream[i]).then_inc(sem(f"ada_landed{i % 2}"), 16)

        s0 = STAGES["ffn0"][0]
        for s in range(RAW, s0 + 4):
            load(s)
            if s in ADA_AFTER:
                for k in range(KC):
                    load_ada(KC * ADA_AFTER[s] + k)

        with sp.Fori(1, FC // 2) as j:
            for u in range(4):
                sp.wait_ge(sem("w_lo_ready"), 4 * j + (s0 + u - RAW + 1))
                sp.dma_start(raw[:, (s0 + u) % RAW, :], wstream[bass.ds(4 * j + (s0 + u), 1)].rearrange("s p n -> p (s n)")
                             ).then_inc(sem(f"raw_landed{(s0 + u) % RAW}"), 16)
                sp.wait_ge(sem("ada_step"), 4 * j + (36 + u - 1))
                sp.dma_start(ada_raw[:, u % 2, :], astream[bass.ds(4 * j + (36 + u), 1)].rearrange("s p n -> p (s n)")
                             ).then_inc(sem(f"ada_landed{u % 2}"), 16)
        for s in range(s0 + 44, s0 + 56):
            load(s)
            if s0 + 46 <= s < s0 + 50 or s >= s0 + 52:
                i = KC * 10 + 2 * (s - s0 - 46) - (4 if s >= s0 + 52 else 0)
                load_ada(i)
                load_ada(i + 1)
        first = STAGES["qc0"][0] + RING
        for s in range(s0 + 56, first):
            load(s)
        sp.wait_ge(sem("xh_act"), 4)
        sp.wait_ge(sem("xh_dve"), 4)
        sp.dma_start(sel_sb[:], dsel).then_inc(sem("in_sel"), 16)
        sp.dma_start(rel_sb[:], rel).then_inc(sem("in_sel"), 16)
        s1 = STAGES["ffn1"][0]
        for s in range(first, s1 + 4):
            load(s)
        with sp.Fori(1, FC // 2) as j:
            for u in range(4):
                sp.wait_ge(sem("w_lo_ready"), 4 * j + (s1 + u - RAW + 1))
                sp.dma_start(raw[:, (s1 + u) % RAW, :], wstream[bass.ds(4 * j + (s1 + u), 1)].rearrange("s p n -> p (s n)")
                             ).then_inc(sem(f"raw_landed{(s1 + u) % RAW}"), 16)
        for s in range(s1 + 44, s1 + 52):
            load(s)
        sp.wait_ge(sem("slot_done"), s1 + 44)
        sp.dma_start(rows_gb[:], ln_rows).then_inc(sem("in_rows"), 16)
        for s in range(s1 + 52, N_SLOTS):
            load(s)
        for tb in range(TB):
            sp.wait_ge(sem("out_ready"), tb + 1)
            sp.dma_start(out[tile_of(tb), :], xh[:, tb, :]).then_inc(sem("stored"), 16)
        sp.wait_ge(sem("stored"), 16 * TB)

    @block.gpsimd
    def _(pool):
        def split(s, slot):
            pool.wait_ge(sem("w_hi_ready"), s + 1)
            nc.gpsimd.tensor_tensor(w_lo[:, slot, :], raw[:, slot % RAW, :], w_hi[:, slot, :].bitcast(F32),
                                    ALU.subtract).then_inc(sem("w_lo_ready"), 1)

        assert RAW == RING
        with pool.Fori(0, N_SLOTS // RING) as i:
            for u in range(RING):
                split(RING * i + u, u)
        for s in range(N_SLOTS // RING * RING, N_SLOTS):
            split(s, s % RING)

    @block.scalar
    def _(act):
        done = [0]

        def to_hi(s, slot, wait_free=True):
            act.wait_ge(sem(f"raw_landed{slot}"), 16 + 16 * (s // RAW) if isinstance(s, int) else 4 * s + (16 - 4 * slot))
            if wait_free:
                act.wait_ge(sem("slot_done"), s - RING + 1)
            nc.scalar.activation(w_hi[:, slot, :], raw[:, slot, :], ACT.Copy).then_inc(sem("w_hi_ready"), 1)

        def hi_until(n):
            for s in range(done[0], min(n, N_SLOTS)):
                to_hi(s, s % RING, s >= RING)
            done[0] = max(done[0], min(n, N_SLOTS))

        def ahead(name):
            hi_until(STAGES[name][0] + STAGES[name][1] + RING - 1)

        def hi_of_chunk(e, n):
            act.wait_ge(sem("h_tmp_ready"), e + 1)
            nc.scalar.activation(h_hi[:, n, :], tmp[:, e % 2, :], ACT.Copy).then_inc(sem("h_hi_ready"), 1)

        def warm_sqrt():
            nc.scalar.activation(warm[:], eps_col, ACT.Sqrt)

        act.wait_ge(sem("in_vec"), 16)
        nc.scalar.activation(c_act[:], vec[:, V_C:V_C + KC], ACT.Silu).then_inc(sem("c_ready"), 1)
        for n in range(KC):
            hi_of_chunk(H_BASE["in"] + n, n)
            if n % 2:
                hi_until(n // 2 + 1)
        hi_until(RING)
        act.wait_ge(sem("in_x0"), 16)
        act.wait_ge(sem("in_x1"), 16)
        for n in range(KC):
            nc.scalar.activation(xa[:, n, :], x_in[:, n, :], ACT.Copy, scale=ALPHA).then_inc(sem("xa_ready"), 1)

        def v_blocks(name, dst):
            for tb in (0, 2):
                part = name if tb == 0 else name + "+"
                wait_full(act, part, 0)
                nc.scalar.activation(dst(tb), v_src(name, tb), ACT.Copy).then_inc(sem("v_act"), 1)

        ahead("narrow")
        wait_full(act, "narrow", 0)
        act.wait_ge(sem("xa_ready"), KC)
        nc.scalar.activation(a_low[:], ps[0:16, pair("narrow"), :], ACT.Copy).then_inc(sem("low_ready"), 1)
        act.wait_ge(sem("row_step"), 2)
        nc.scalar.activation(rows[:, 1, :], rows[:, 1, :], ACT.Exp).then_inc(sem("row_act"), 1)
        act.wait_ge(sem("row_act"), 1)
        nc.scalar.activation(rows[:, 1, :], rows[:, 1, :], ACT.Ln, bias=1.0).then_inc(sem("row_act"), 1)
        ahead("va")
        v_blocks("va", v_dst["va"])
        step, prep = sem("prep_act"), sem("prep_dve")
        for p in range(2):
            act.wait_ge(prep, 2 * p + 2)
            nc.scalar.activation(t1[:, p, :], t1[:, p, :], ACT.Exp).then_inc(step, 1)
        for p in range(2):
            act.wait_ge(step, p + 1)
            nc.scalar.activation(t1[:, p, :], t1[:, p, :], ACT.Ln, bias=1.0).then_inc(step, 1)
        for p in range(2):
            act.wait_ge(prep, 2 * p + 6)
            nc.scalar.activation(t1[:, p, :], scan_b[:, p, :], ACT.Exp, scale=1 / TAU).then_inc(step, 1)
            nc.scalar.activation(dec[:, p, :], scan_b[:, p, CHUNK - 1::CHUNK], ACT.Exp, scale=1 / TAU)
            nc.scalar.activation(t3[:, p, :], scan_b[:, p, :], ACT.Exp, scale=-1 / TAU).then_inc(step, 1)
        for p in range(2):
            act.wait_ge(prep, p + 9)
            nc.scalar.activation(t2[:, p, :], t2[:, p, :], ACT.Exp, scale=1 / TAU).then_inc(step, 1)
        ahead("qa")
        ahead("ka")
        act.wait_ge(sem("am_copied"), 1)
        nc.scalar.activation(em_col, ps[:, 6, 16:32], ACT.Exp, scale=-1.0).then_inc(sem("em_ready"), 1)

        for p in range(4):
            name = f"qkb{p}"
            ahead(name)
            for b in range(2):
                ch = 2 * p + b
                wait_full(act, name, b)
                if ch >= CONV_RING:
                    act.wait_ge(sem("conv_done"), ch - CONV_RING + 1)
                else:
                    act.wait_ge(sem("pads_ready"), 1)
                nc.scalar.activation(q_raw[:, ch % CONV_RING, 3:3 + S], ps[:, pair(name) + b, :], ACT.Copy).then_inc(sem("conv_in"), 1)
            for b in range(2):
                ch = 2 * p + b
                act.wait_ge(sem("conv_done"), ch + 1)
                nc.scalar.activation(qk[:, ch, :], tmp[:, b, :], ACT.Silu).then_inc(sem("qk_ready"), 1)
            if p == 0:
                for k in range(2):
                    act.wait_ge(sem("kd_full"), k + 1)
                    nc.scalar.activation(kdt[:, :, k, :], ps[:, 4 + k, :].rearrange("q (t d) -> q t d", t=TB), ACT.Copy
                                         ).then_inc(sem("kd_ready"), 1)

        ahead("vb")
        v_blocks("vb", v_dst["vb"])
        for name, func, col in (("ra", ACT.Silu, 0), ("ob", ACT.Sigmoid, S)):
            ahead(name)
            for tb in range(TB):
                part, b = (name, tb) if tb < 2 else (name + "+", tb - 2)
                wait_full(act, part, b)
                nc.scalar.activation(og[:, tb, col:col + S], ps[:, pair(part) + b, :], func).then_inc(sem(f"{name}_ready"), 1)
            if name == "ra":
                act.wait_ge(sem("o_done"), TB)
                nc.scalar.activation(cols[:, 5, :], mv[:, :, 1], ACT.Sqrt, bias=eps_col).then_inc(sem("std_gla"), 1)

        def ml_weights(h):
            act.wait_ge(sem("ed_ready"), h + 1)
            if h == 0:
                act.wait_ge(sem("pv_free"), 1)
            if h >= 2:
                act.wait_ge(sem("ml_a_ready"), h - 1)
            for j in range(TB):
                bias = a_col[:, j * 4 + h:j * 4 + h + 1]
                i = nc.scalar.activation(ml_w[:, h % 2, OFS[j]:OFS[j] + P], tmp[:, h % 2, tile_of(j)], ACT.Exp, bias=bias)
                if j < TB - 1:
                    i = nc.scalar.activation(ml_w[:, h % 2, OFS[j] + P:OFS[j] + WID[j]],
                                             ps[:, NG_BANK[h % 2], (j + 1) * P:S], ACT.Exp, bias=bias)
            i.then_inc(sem("ml_w_ready"), 1)

        def ml_out(h):
            act.wait_ge(sem("num_full"), h + 1)
            for b in range(2):
                i = nc.scalar.activation(num[:, h, 2 * b:2 * b + 2, :],
                                         ps[:, 4 + b, 0:258].rearrange("q (t d) -> q t d", t=2), ACT.Copy)
            i.then_inc(sem("num_ready"), 1)

        ml_weights(0)
        ml_weights(1)
        for h in range(4):
            ml_out(h)
            if h + 2 < 4:
                ml_weights(h + 2)
            if h == 2:
                warm_sqrt()
        act.wait_ge(sem("num_ready"), 4)
        nc.scalar.activation(cols[:, 2, :], num[:, :, :, 128].rearrange("q h t -> q (h t)"), ACT.Abs).then_inc(sem("den_abs"), 1)
        act.wait_ge(sem("ml_var"), 1)
        nc.scalar.activation(cols[:, 4, :], cols[:, 4, :], ACT.Sqrt, bias=eps_col).then_inc(sem("ml_std"), 1)
        for n in range(KC):
            hi_of_chunk(H_BASE["cat0"] + n, n)

        def norm(i, names, rt):
            for n in range(KC):
                ahead(names[n // 2])
                act.wait_ge(sem("rt_full"), KC * i + n + 1)
                nc.scalar.activation(rt[:, :, tile_of(n)], ps[:, 4 + n % 2, :].rearrange("q (t d) -> q t d", t=TB),
                                     ACT.Copy).then_inc(sem("rt_ready"), 1)
                if n == 5:
                    warm_sqrt()
            act.wait_ge(sem("mv_ready"), i + 1)
            nc.scalar.activation(cols[:, 5, 0:TB], mv[:, 0:TB, 1], ACT.Sqrt, bias=eps_col).then_inc(sem("std_ready"), 1)
            act.wait_ge(sem("nmr_ready"), i + 1)
            for tb in (1, 3):
                nc.scalar.activation(xh[:, tb, :], rt[:, tb, :], ACT.Identity, scale=rstd[:, tb:tb + 1], bias=nmr[:, tb:tb + 1]
                                     ).then_inc(sem("xh_act"), 1)
            if i == 3:
                return
            for n in range(KC):
                hi_of_chunk(H_BASE[f"norm{i}"] + n, n)
                nc.scalar.activation(xa[:, n, :], ps[:, pair(f"norm{i}_{n // 2}") + n % 2, :], ACT.Identity,
                                     scale=lnga[:, i, n:n + 1], bias=lnba[:, i, n:n + 1]).then_inc(sem("xa_ready"), 1)

        def ffn(layer):
            s0 = STAGES[f"ffn{layer}"][0]
            f0 = uses[where[f"gate{layer}_0"]][1][0][1]
            gate = pair(f"gate{layer}_0")

            def step(j, first=False):
                for s in (3, 4):
                    to_hi(4 * j + (s0 + s), (s0 + s) % RING)
                for b in range(2):
                    act.wait_ge(*((sem("bank_full"), 2 * j + f0) if b == 0 else (sem("slot_done"), 4 * j + (s0 + 2))))
                    if first:
                        act.wait_ge(sem("h_ready"), H_BASE[f"norm{2 * layer}"] + KC)
                    else:
                        act.wait_ge(sem("hid_ready"), 2 * j + (FC * layer - 1 + b))
                    nc.scalar.activation(tmp[:, b, :], ps[:, gate + b, :], ACT.Silu).then_inc(sem("silu_ready"), 1)
                for s in (5, 6):
                    to_hi(4 * j + (s0 + s), (s0 + s) % RING)
                for b in range(2):
                    act.wait_ge(sem("prod_ready"), 2 * j + (FC * layer + 1 + b))
                    dst = hid_hi[:, b, :] if first else hid_hi[:, bass.ds(2 * j + b, 1), :].rearrange("p o t -> p (o t)")
                    nc.scalar.activation(dst, tmp[:, b, :], ACT.Copy).then_inc(sem("hid_hi_ready"), 1)

            hi_until(s0 + 3)
            step(0, True)
            with act.Fori(1, FC // 2) as j:
                step(j)
            done[0] = s0 + 4 * (FC // 2) + 3

        norm(0, [f"out0{p}" for p in range(4)], rt_mixer)
        ffn(0)
        norm(1, [f"down0{p}" for p in range(4)], rt_ffn)

        def qk_panel(part):
            name, p = part[:2], int(part[2])
            ahead(part)
            wait_full(act, part, 0)
            src = ps[:, pair(part), :]
            o = {"qc": qc, "kc": kc, "qd": qd, "kd": kd}[name][:, 2 * p, :]
            if name[1] == "d" and p >= 1:
                o, src = o.rearrange("q (t p) -> q t p", t=RES), by_residue(src)
            nc.scalar.activation(o, src, ACT.Copy, scale=0.125 if name[0] == "q" else 1.0).then_inc(sem("qk1_act"), 1)

        for part in ("qc0", "qc1", "kc0", "kc1"):
            qk_panel(part)
        act.wait_ge(sem("f_ready"), 1)
        act.dma_start(f_dram.rearrange("(h g) x -> h g x", h=4), f_rows[:]).then_inc(sem("f_stored"), 16)
        ahead("vc")
        v_blocks("vc", v_dst["vc"])
        act.wait_ge(sem("f_stored"), 16)
        skew_rows(act)

        def sb_first(h):
            z = psf[:, sb_col(h):sb_col(h) + SC]
            a = sb_a[h % 2]
            act.wait_ge(sem("z_full"), h + 1)
            if h >= 2:
                act.wait_ge(sem("av_done"), h - 1)
            nc.scalar.activation(a[:], z, ACT.Abs).then_inc(sem("sb_act"), 1)
            act.wait_ge(sem("sb_act"), 3 * h + 1)
            nc.scalar.activation(a[:], a[:], ACT.Exp, scale=-1.0).then_inc(sem("sb_act"), 1)
            act.wait_ge(sem("sb_act"), 3 * h + 2)
            nc.scalar.activation(a[:], a[:], ACT.Ln, bias=1.0).then_inc(sem("sb_act"), 1)

        def sb_second(h):
            act.wait_ge(sem("tri_full"), h + 1)
            nc.scalar.activation(sb_a[h % 2][:], psf[:, sb_col(h):sb_col(h) + SC], ACT.Exp).then_inc(sem("att_exp"), 1)

        sb_first(0)
        for i, part in enumerate(FILL):
            if part[0] == "v":
                ahead(part)
                v_blocks(part, v_dst[part])
            else:
                qk_panel(part)
            if i == 1:
                act.wait_ge(sem("skewed"), 16)
                load_bias(act)
            if i % 2 == 0:
                sb_second(i // 2)
            else:
                sb_first(i // 2 + 1)
        hi_of_chunk(H_BASE["cat1"], 0)
        for h in range(4, 8):
            if h + 1 < 8:
                sb_first(h + 1)
            sb_second(h)
            if h % 2 == 0:
                hi_of_chunk(H_BASE["cat1"] + h // 2 - 1, h // 2 - 1)
        hi_of_chunk(H_BASE["cat1"] + 3, 3)

        def dil_exp(h, kind):
            act.wait_ge(sem("nm_ready"), 1)
            for t in range(TB):
                i = nc.scalar.activation(lgs[kind][:, h, t, :], lgs[kind][:, h, t, :], ACT.Exp,
                                         bias=nm[:, kind, TB * t + h:TB * t + h + 1])
            i.then_inc(sem("dil_p"), 1)

        dil_exp(0, 0)
        dil_exp(0, 1)
        for n in range(0, 16, 2):
            act.wait_ge(sem("turn_full"), n + 1)
            if n >= 4:
                act.wait_ge(sem("pv_done"), n - 3)
            nc.scalar.activation(pt[:, n % 4, :], ps[:, n % 4, :], ACT.Copy).then_inc(sem("turn_act"), 1)
            if n // 4 + 1 < 4:
                dil_exp(n // 4 + 1, n % 4 // 2)
            if n == 10:
                hi_of_chunk(H_BASE["cat1"] + 4, 4)
        hi_of_chunk(H_BASE["cat1"] + 5, 5)
        norm(2, [f"out1{p}" for p in range(4)], rt_mixer)
        ffn(1)
        norm(3, [f"down1{p}" for p in range(4)], rt_ffn)

    @block.tensor
    def _(pe):
        def slot_waits(s):
            pe.wait_ge(sem("w_hi_ready"), s + 1)
            pe.wait_ge(sem("w_lo_ready"), s + 1)

        def mm3(o, w_h, w_l, x_h, x_l, start, stop):
            pe.matmul(o, w_h, x_l, start=start, stop=False)
            pe.matmul(o, w_h, x_h, start=False, stop=False)
            return pe.matmul(o, w_l, x_h, start=False, stop=stop)

        def wpart(w, s, kk, b):
            return w[:, s % RING, kk * 256 + b * P:kk * 256 + (b + 1) * P]

        def panel(name, nk, x_h, x_l, ready=None):
            wait_pair(pe, name)
            first = STAGES[name][0]
            bank = pair(name)
            for i, (k0, n) in enumerate(panel_slots(nk)):
                s = first + i
                slot_waits(s)
                for b in range(2):
                    for kk in range(n):
                        k = k0 + kk
                        if ready and b == 0:
                            pe.wait_ge(sem(ready[0]), ready[1] + k + 1)
                        m = mm3(ps[:, bank + b, :], wpart(w_hi, s, kk, b), wpart(w_lo, s, kk, b), x_h[:, k, :], x_l[:, k, :],
                                k == 0, k == nk - 1)
                        if b == 0 and k == nk - 1:
                            m.then_inc(sem("bank_full"), 1)
                m.then_inc(sem("slot_done"), 1)

        def group(name, kk_n, width):
            first, count = STAGES[name]
            wait_pair(pe, name)
            for i in range(count):
                s = first + i
                slot_waits(s)
                for tb in range(TB):
                    part, b = (name, tb) if tb < 2 else (name + "+", tb - 2)
                    if i == 0 and tb == 2:
                        wait_pair(pe, part)
                    o = ps[:, pair(part) + b, 0:width]
                    tokens = slice(tb, S, RES) if name == "vd0" else tile_of(tb)
                    for kk in range(kk_n):
                        k = i * kk_n + kk
                        w = slice(kk * width, (kk + 1) * width)
                        start, stop = k == 0, k == KC - 1
                        pe.matmul(o, h_lo[:, k, tokens], w_hi[:, s % RING, w], start=start, stop=False)
                        pe.matmul(o, h_hi[:, k, tokens], w_hi[:, s % RING, w], start=False, stop=False)
                        m = pe.matmul(o, h_hi[:, k, tokens], w_lo[:, s % RING, w], start=False, stop=stop)
                    if i == count - 1 and tb < TB - 1:
                        m.then_inc(sem("bank_full"), 1)
                m.then_inc(sem("slot_done"), 1)

        def ada_cols(blk):
            pe.wait_ge(sem("ada_step"), KC * (blk + 1) if isinstance(blk, int) else KC * blk + KC)
            for n in range(KC):
                m = pe.matmul(ps[:, 7, n:n + 1], ada_acc[:, tile_of(n)], one_col, start=True, stop=True)
            m.then_inc(sem("ada_cols"), 1)

        pe.wait_ge(sem("in_const"), 16)
        ada_cols(0)
        pe.wait_ge(sem("mod_ready"), 1)
        ada_cols(1)

        slot_waits(0)
        for k in range(KC):
            pe.wait_ge(sem("h_ready"), H_BASE["in"] + k + 1)
            m = mm3(ps[0:96, 0, :], w_hi[:, 0, k * P:k * P + 96], w_lo[:, 0, k * P:k * P + 96], h_hi[:, k, :], h_lo[:, k, :],
                    k == 0, k == KC - 1)
        m.then_inc(sem("bank_full"), 1)
        pe.wait_ge(sem("bank_full"), 1)
        pe.sem_inc(sem("slot_done"), 1)
        group("va", 2, S)
        pe.wait_ge(sem("in_mcon"), 32)
        pe.wait_ge(sem("low_ready"), 1)
        for p in range(2):
            m = pe.matmul(ps[:, 4 + p, :], mcon[0:16, M_WAUP + p * P:M_WAUP + (p + 1) * P], a_low[:], start=True, stop=True)
        m.then_inc(sem("gate_full"), 1)
        ada_cols(2)
        panel("qa", KC, h_hi, h_lo)
        panel("ka", KC, h_hi, h_lo)
        pe.wait_ge(sem("row_step"), 4)
        for k, r in ((0, 0), (1, 2)):
            for tb in range(TB):
                m = pe.transpose(ps[:, 6, 16 * k + 4 * tb:16 * k + 4 * tb + 4], rows[:, r, tile_of(tb)], ident[0:4, 0:4])
        m.then_inc(sem("am_full"), 1)
        panel("qkb0", KC, h_hi, h_lo)
        for p in range(2):
            pe.wait_ge(sem("prep_dve"), 2 * p + 14)
            for tb in range(TB):
                m = pe.transpose(ps[:, 4 + p, tile_of(tb)], tmp[:, p, tile_of(tb)], ident)
            m.then_inc(sem("kd_full"), 1)
        panel("qkb1", KC, h_hi, h_lo)
        for h in range(4):
            p, e = divmod(h, 2)
            if h == 0:
                pe.wait_ge(sem("kd_ready"), 2)
            if h == 2:
                pe.wait_ge(sem("em_ready"), 1)
            if h == 3:
                pe.wait_ge(sem("mod_ready"), 3)
            for tb in range(TB):
                m = pe.matmul(ps[:, GLA_BANK[h], tile_of(tb)], k_in[64 * e:64 * e + 64, p, tile_of(tb)],
                              q_in[64 * e:64 * e + 64, p, tile_of(tb)], start=True, stop=True)
            m.then_inc(sem("gla_s_full"), 1)
        panel("qkb2", KC, h_hi, h_lo)

        def chunk_sums(p):
            for c in range(NCH - 1):
                if c == 0:
                    pe.wait_ge(*((sem("gla_p_ready"), 4) if p == 0 else (sem("st_ready"), 7)))
                if c == 0:
                    pe.wait_ge(sem("v_dve"), 2)
                r = 64 * (c % 2)
                m = pe.matmul(ps[:, KV_BANK[c], (c // 2 % 2) * 256:(c // 2 % 2) * 256 + 256], kdt[r:r + 64, c // 2, p, :],
                              va[r:r + 64, c // 2, p * 256:(p + 1) * 256], start=True, stop=True, skip_group_check=True)
                if c in (3, 6):
                    m.then_inc(sem("kv_full"), 1)

        chunk_sums(0)
        panel("qkb3", KC, h_hi, h_lo)
        chunk_sums(1)
        group("vb", 2, S)
        group("ra", 2, S)
        ada_cols(3)
        pe.wait_ge(sem("st_ready"), 14)
        for tb in range(TB):
            if tb == 3:
                pe.wait_ge(sem("o_done"), 1)
            bank = O_BANK[tb]
            for h in range(4):
                pe.matmul(ps[:, bank, tile_of(h)], gla_p[:, h, tile_of(tb)], va[:, tb, tile_of(h)],
                          start=h == 0, stop=False, skip_group_check=True)
            for h in (0, 2, 1, 3):
                p, e = divmod(h, 2)
                if h == 1:
                    m.then_inc(sem("lower_done"), 1)
                    pe.wait_ge(sem("lower_done"), tb + 1)
                for c in (2 * tb, 2 * tb + 1):
                    if c:
                        r = 64 * (c % 2)
                        m = pe.matmul(ps[r:r + 64, bank, tile_of(h)], q_in[64 * e:64 * e + 64, p, c * CHUNK:(c + 1) * CHUNK],
                                      st[64 * e:64 * e + 64, p, c - 1, :], start=False, stop=True, skip_group_check=True)
            m.then_inc(sem("o_full"), 1)
        group("ob", 2, S)

        def neg_rows(h):
            if h >= 2:
                pe.wait_ge(sem("ml_w_ready"), h - 1)
            pe.matmul(ps[:, NG_BANK[h % 2], :], mcon[0:4, M_SEL + h * P:M_SEL + (h + 1) * P], neg_g[:],
                      start=True, stop=True).then_inc(sem("ng_full"), 1)

        def ml_scores(h):
            if h == 0:
                pe.wait_ge(sem("qk_ready"), KC)
            if h >= 1:
                pe.wait_ge(sem("ml_a_ready"), h)
            for j in range(TB):
                m = pe.matmul(psf[:, OFS[j]:OFS[j] + WID[j]], qk[:, 4 + h, tile_of(j)], qk[:, h, j * P:S],
                              start=True, stop=True, skip_group_check=True)
            m.then_inc(sem("ml_s_full"), 1)

        def ml_num(h):
            pe.wait_ge(sem("ml_a_ready"), h + 1)
            if h == 0:
                pe.wait_ge(sem("v_dve"), 4)
            if h >= 1:
                pe.wait_ge(sem("num_ready"), h)
            for tb in range(TB):
                o = ps[:, 4 + tb // 2, (tb % 2) * 129:(tb % 2) * 129 + 129]
                for j in range(tb + 1):
                    m = pe.matmul(o, ml_a[:, h % 2, OFS[j] + (tb - j) * P:OFS[j] + (tb - j + 1) * P], vb[:, j, h, :],
                                  start=j == 0, stop=j == tb, skip_group_check=True)
            m.then_inc(sem("num_full"), 1)

        wait_free(pe, "ob")
        wait_free(pe, "ob+")
        pe.wait_ge(sem("o_done"), TB)
        neg_rows(0)
        ml_scores(0)
        neg_rows(1)
        ml_scores(1)
        neg_rows(2)
        ml_num(0)
        ml_scores(2)
        neg_rows(3)
        ml_num(1)
        ml_scores(3)
        ml_num(2)
        ml_num(3)

        def turn_in(e, n, src, ready):
            pe.wait_ge(*ready)
            if n >= 2:
                pe.wait_ge(sem("h_tmp_ready"), e - 1)
            for tb in range(TB):
                m = pe.transpose(ps[:, 4 + n % 2, tile_of(tb)], src(tb), ident)
            m.then_inc(sem("cat_full"), 1)

        pe.wait_ge(sem("num_ready"), 4)
        for n in range(KC):
            turn_in(H_BASE["cat0"] + n, n, lambda tb: og[:, tb, tile_of(n)], (sem("og_ready"), 1 if n < 4 else n - 2))
        for p in range(4):
            panel(f"out0{p}", KC, h_hi, h_lo, ("h_ready", H_BASE["cat0"]) if p == 0 else None)
            turn_out(pe, 0, p)
            if p == 1:
                ada_cols(4)

        def turn_back(i):
            for n in range(KC):
                name = f"norm{i}_{n // 2}"
                if n % 2 == 0:
                    wait_pair(pe, name)
                for tb in range(TB):
                    if n == 0:
                        pe.wait_ge(sem("xh_act" if tb % 2 else "xh_dve"), 2 * i + tb // 2 + 1)
                    m = pe.transpose(ps[:, pair(name) + n % 2, tile_of(tb)], xh[:, tb, tile_of(n)], ident)
                m.then_inc(sem("bank_full"), 1)

        def ffn(layer):
            s0 = STAGES[f"ffn{layer}"][0]
            i = where[f"gate{layer}_0"]

            def step(j, first=False):
                for m_ in range(2):
                    bank = pair(f"gate{layer}_0") if m_ == 0 else pair(f"up{layer}_0")
                    if first:
                        wait_pair(pe, f"gate{layer}_0" if m_ == 0 else f"up{layer}_0")
                    else:
                        pe.wait_ge(sem("silu_ready" if m_ == 0 else "prod_ready"), 2 * j + FC * layer)
                    for half in range(2):
                        u = 2 * m_ + half
                        s = s0 + u
                        slot_waits(4 * j + s)
                        for b in range(2):
                            for kk in range(4):
                                k = 4 * half + kk
                                if first and m_ == 0 and b == 0:
                                    pe.wait_ge(sem("h_ready"), H_BASE[f"norm{2 * layer}"] + k + 1)
                                m = mm3(ps[:, bank + b, :], wpart(w_hi, s, kk, b), wpart(w_lo, s, kk, b),
                                        h_hi[:, k, :], h_lo[:, k, :], k == 0, k == KC - 1)
                                if b == 0 and k == KC - 1:
                                    m.then_inc(sem("bank_full"), 1)
                        m.then_inc(sem("slot_done"), 1)

            assert uses[i][0] != uses[i + 1][0]
            step(0, True)
            if layer == 0:
                with pe.Fori(0, FC // 4) as it:
                    step(2 * it + 1)
                    step(2 * it + 2)
                    ada_cols(it + 5)
            else:
                with pe.Fori(1, FC // 2) as j:
                    step(j)
            for p in range(4):
                if layer == 0 and p == 1:
                    ada_cols(10)
                panel(f"down{layer}{p}", FC, hid_hi, hid_lo, ("hid_ready", FC * layer) if p == 0 else None)
                turn_out(pe, 2 * layer + 1, p)
            if layer == 0:
                ada_cols(11)

        turn_back(0)
        ffn(0)
        turn_back(1)

        for name in ("qc", "kc"):
            for p in range(2):
                panel(f"{name}{p}", KC, h_hi, h_lo, ("h_ready", H_BASE["norm1"]) if name == "qc" and p == 0 else None)
            if name == "qc":
                pe.wait_ge(sem("in_sel"), 32)
                for g in range(3):
                    m = pe.matmul(ps[0:4, 4 + g, 0:F_LEN], rel_sb[:, 4 * g:4 * g + 4], sel_sb[:, g, :], start=True, stop=True)
                m.then_inc(sem("f_full"), 1)
        group("vc", 2, S)

        def sb_z(h):
            c, r = h // 2, 64 * (h % 2)
            base = sb_col(h)
            if h == 0:
                pe.wait_ge(sem("f_ready"), 1)
            elif h <= 4:
                pe.wait_ge(sem("att_exp"), h)
            elif h >= 6:
                pe.wait_ge(sem("att_exp"), h - 1)
            for j in (0, 1, 2, 3):
                m = pe.matmul(psf[:, base + OFS[j]:base + OFS[j] + WID[j]], kc[r:r + 64, c, tile_of(j)], qc[r:r + 64, c, j * P:S],
                              start=j < 3, stop=False, skip_group_check=True)
            m.then_inc(sem("z_full"), 1)

        def sb_tri(h):
            base = sb_col(h)
            sp_ = sb_sp[h % 2]
            pe.wait_ge(sem("sp_ready"), h + 1)
            for j in range(TB):
                pe_out = psf[:, base + OFS[j]:base + OFS[j] + WID[j]]
                m = pe.matmul(pe_out, cst[:, C_TRI:C_TRI + P], sp_[:, OFS[j]:OFS[j] + WID[j]], start=False,
                              stop=j == TB - 1, skip_group_check=True)
                for k in range(j + 1, TB):
                    m = pe.matmul(psf[:, base + OFS[j] + (k - j) * P:base + OFS[j] + WID[j]], cst[:, C_ONES:C_ONES + P],
                                  sp_[:, OFS[k]:OFS[k] + WID[k]], start=False, stop=k == TB - 1, skip_group_check=True)
            m.then_inc(sem("tri_full"), 1)

        def sb_av(h):
            c, r = h // 2, 64 * (h % 2)
            pe.wait_ge(sem("att_ready"), h + 1)
            if h == 0:
                pe.wait_ge(sem("mod_ready"), 13)
            if h == 2:
                pe.wait_ge(sem("staged"), 1)
            if h == 4:
                pe.wait_ge(sem("h_tmp_ready"), H_BASE["cat1"] + 2)
            for j in range(TB):
                m = pe.matmul(ps[r:r + 64, AV_BANK[c], j * P:S], vc[:, j, h * 64:h * 64 + 64], sb_a[h % 2][:, OFS[j]:OFS[j] + WID[j]],
                              start=j == 0, stop=j == TB - 1, skip_group_check=True)
            m.then_inc(sem("av_done"), 1)

        sb_z(0)
        for i, part in enumerate(FILL):
            if part[0] == "v":
                group(part, 2 if part == "vd0" else 4, S if part == "vd0" else 256)
            else:
                panel(part, KC, h_hi, h_lo)
            if i % 2 == 0:
                sb_tri(i // 2)
            elif i < 7:
                sb_av(i // 2)
                sb_z(i // 2 + 1)
        sb_z(4)
        wait_free(pe, "vd1")
        wait_free(pe, "vd1+")
        for h in range(4, 8):
            if h + 1 < 8:
                sb_z(h + 1)
            sb_av(h - 1)
            sb_tri(h)
        sb_av(7)

        pe.wait_ge(sem("att_exp"), 8)
        for s in range(16):
            h, part = score_step(s)
            g = (1, 2, 0, 0)[part]
            hd = g * 4 + h
            r = 64 * (h % 2)
            if s >= 4:
                pe.wait_ge(sem("l_read"), s - 3)
            for t in part_tiles(part):
                m = pe.matmul(ps[:, score_bank(s), tile_of(t)], qd[r:r + 64, hd // 2, tile_of(t)],
                              kd[r:r + 64, hd // 2, tile_of(t - 1 if part == 3 else t)], start=True, stop=True,
                              skip_group_check=True)
            m.then_inc(sem("l_full"), 1)
        pe.wait_ge(sem("dil_mx"), 1)
        for kind in range(2):
            for t in range(TB):
                o = ps[0:4, 4 + kind, t:S:RES] if kind == 0 else ps[0:4, 4 + kind, tile_of(t)]
                m = pe.transpose(o, mx[:, kind, TB * t:TB * t + 4], ident)
        m.then_inc(sem("mx_turned"), 1)
        pe.wait_ge(sem("m_rows_ready"), 1)
        for kind in range(2):
            for t in range(TB):
                src = m_rows[:, t:S:RES] if kind == 0 else m_rows[:, tile_of(t)]
                m = pe.transpose(ps[:, 4, 16 * kind + 4 * t:16 * kind + 4 * t + 4], src, ident[0:4, 0:4])
        m.then_inc(sem("m_turned"), 1)

        def turn_round(n):
            h, part = divmod(n, 4)
            pe.wait_ge(sem("dil_p"), 2 * h + 1 + part // 2)
            if n >= 4:
                pe.wait_ge(sem("turn_dve" if n % 2 else "turn_act"), (n - 4) // 2 + 1)
            for t in range(TB):
                m = pe.transpose(ps[:, n % 4, tile_of(t)], lgs[part // 2][:, h, t, (0, P, P, 0)[part]:][:, 0:P], ident)
            m.then_inc(sem("turn_full"), 1)

        def pv_round(n):
            h, part = divmod(n, 4)
            g = (1, 2, 0, 0)[part]
            pe.wait_ge(sem("turn_dve" if n % 2 else "turn_act"), n // 2 + 1)
            if part == 0 and h >= 2:
                pe.wait_ge(*((sem("dil_out"), 1) if h == 2 else (sem("h_tmp_ready"), H_BASE["cat1"] + 5)))
            for t in part_tiles(part):
                key = t - 1 if part == 3 else t
                v1 = vd[:, key, (g - 1) % 3 * 2 + h // 2, h % 2:h % 2 + 2, :].rearrange("q a d -> q (a d)")
                o = ps[:, 6 + h % 2, t:S:RES] if g else ps[:, 6 + h % 2, tile_of(t)]
                m = pe.matmul(o, v1, pt[:, n % 4, tile_of(t)], start=part == 0 and t == 0, stop=part == 3 and t == TB - 1,
                              skip_group_check=True)
            m.then_inc(sem("pv_done"), 1)

        pe.wait_ge(sem("h_tmp_ready"), H_BASE["cat1"] + 4)
        for n in range(3):
            turn_round(n)
        for n in range(16):
            pv_round(n)
            if n + 3 < 16:
                turn_round(n + 3)
        for p in range(4):
            panel(f"out1{p}", 6, h_hi, h_lo, ("h_ready", H_BASE["cat1"]) if p == 0 else None)
            turn_out(pe, 2, p)
        turn_back(2)
        ffn(1)

    @block.vector
    def _(dve):
        chain = [0]
        V = nc.vector

        def link(ins):
            chain[0] += 1
            ins.then_inc(sem("dve_chain"), 1)
            dve.wait_ge(sem("dve_chain"), chain[0])

        def vcol(c, n=1):
            return vec[:, c:c + n]

        def lo_of_chunk(e, n):
            dve.wait_ge(sem("h_hi_ready"), e + 1)
            V.tensor_tensor(h_lo[:, n, :], tmp[:, e % 2, :], h_hi[:, n, :].bitcast(F32), ALU.subtract).then_inc(sem("h_ready"), 1)

        def tmp_free(e):
            if e >= 2:
                dve.wait_ge(sem("h_ready"), e - 1)

        def ada_slot(i, src, first):
            k = i % KC
            if first:
                if i:
                    dve.wait_ge(sem("ada_step"), i)
                V.tensor_scalar(ada_acc[:], src, c_act[:, k:k + 1], None, ALU.mult).then_inc(sem("ada_step"), 1)
            else:
                dve.wait_ge(sem("ada_step"), i)
                V.scalar_tensor_tensor(ada_acc[:], src, c_act[:, k:k + 1], ada_acc[:], ALU.mult, ALU.add
                                       ).then_inc(sem("ada_step"), 1)

        def mod_block(blk):
            dve.wait_ge(sem("ada_cols"), blk + 1)
            V.tensor_tensor(mod[:, blk, :], ps[:, 7, 0:KC], vcol(V_ADAB + blk * KC, KC), ALU.add).then_inc(sem("mod_ready"), 1)

        def ada_block(blk, before=True, ks=range(KC)):
            if blk > 2 and before:
                mod_block(blk - 1)
            for k in ks:
                i = KC * blk + k
                dve.wait_ge(sem(f"ada_landed{i % 2}"), 16 * ((i - 16) // 2 + 1))
                ada_slot(i, ada_raw[:, i % 2, :], k == 0)

        def derive(i, blk_shift, blk_scale, ln):
            if ln is None:
                V.tensor_scalar(scl[:, i, :], mod[:, blk_scale, :], 1.0, None, ALU.add)
                link(V.tensor_copy(bia[:, i, :], mod[:, blk_shift, :]))
                return
            V.scalar_tensor_tensor(scl[:, i, :], mod[:, blk_scale, :], 1.0, vcol(V_LNG + ln * KC, KC), ALU.add, ALU.mult)
            link(V.scalar_tensor_tensor(bia[:, i, :], mod[:, blk_scale, :], 1.0, vcol(V_LNB + ln * KC, KC), ALU.add, ALU.mult))
            link(V.tensor_tensor(bia[:, i, :], bia[:, i, :], mod[:, blk_shift, :], ALU.add))

        dve.wait_ge(sem("c_ready"), 1)
        for blk in range(2):
            if blk:
                mod_block(0)
            for k in range(KC):
                i = KC * blk + k
                dve.wait_ge(sem(f"in_ada{i // 4}"), 16)
                ada_slot(i, ada_first[:, i, :], k == 0)
        mod_block(1)
        dve.wait_ge(sem("mod_ready"), 2)
        derive(0, 0, 1, None)
        V.memset(eps_col, EPS)
        V.tensor_scalar(lnga[:], vcol(V_LNG, 32).rearrange("p (a b) -> p a b", a=4), ALPHA, None, ALU.mult)
        link(V.tensor_scalar(lnba[:], vcol(V_LNB, 32).rearrange("p (a b) -> p a b", a=4), ALPHA, None, ALU.mult))
        dve.wait_ge(sem("in_x0"), 16)

        def chunk_from(e, n, src, i):
            tmp_free(e)
            V.tensor_scalar(tmp[:, e % 2, :], src, scl[:, i, n:n + 1], bia[:, i, n:n + 1], ALU.mult, ALU.add
                            ).then_inc(sem("h_tmp_ready"), 1)

        for n in range(KC):
            if n == 4:
                dve.wait_ge(sem("in_x1"), 16)
            chunk_from(n, n, x_in[:, n, :], 0)
            if n >= 1:
                lo_of_chunk(n - 1, n - 1)
        lo_of_chunk(KC - 1, KC - 1)
        dve.wait_ge(sem("xa_ready"), KC)
        V.memset(vb[:, :, :, 128:129], 1.0)

        wait_full(dve, "narrow", 0)
        fps, ips = ps[64:68, 0, :], ps[32:36, 0, :]
        V.tensor_scalar(rows[:, 1, :], fps, vec[64:68, V_BF:V_BF + 1], 0.0, ALU.add, ALU.max)
        V.tensor_scalar(rows[:, 2, :], fps, vec[64:68, V_BF:V_BF + 1], 0.0, ALU.add, ALU.min).then_inc(sem("row_step"), 1)
        dve.wait_ge(sem("row_step"), 1)
        V.tensor_tensor(rows[:, 1, :], rows[:, 2, :], rows[:, 1, :], ALU.subtract).then_inc(sem("row_step"), 1)
        V.tensor_scalar(rows[:, 0, :], ips, vec[32:36, V_BI:V_BI + 1], None, ALU.add).then_inc(sem("row_step"), 1)
        prep = sem("prep_dve")

        dve.wait_ge(sem("row_act"), 2)
        link(V.tensor_tensor(rows[:, 2, :], rows[:, 2, :], rows[:, 1, :], ALU.subtract))
        link(V.tensor_tensor_scan(rows[:, 1, :], rows[:, 2, :], rows[:, 2, :], 0.0, ALU.add, ALU.min))
        link(V.tensor_tensor(rows[:, 0, :], rows[:, 0, :], rows[:, 1, :], ALU.subtract))
        link(V.tensor_tensor_scan(rows[:, 3, :], rows[:, 0, :], rows[:, 0, :], 0.0, ALU.max, ALU.max))
        V.tensor_scalar(neg_g[:], rows[:, 3, :], -1.0, None, ALU.mult)
        V.tensor_tensor(rows[:, 2, :], rows[:, 1, :], rows[:, 3, :], ALU.add).then_inc(sem("row_step"), 1)

        def v_blocks(name):
            for tb in (1, 3):
                part = name if tb == 1 else name + "+"
                wait_full(dve, part, 1)
                V.tensor_copy(v_dst[name](tb), v_src(name, tb)).then_inc(sem("v_dve"), 1)

        ada_block(2)
        v_blocks("va")
        dve.wait_ge(sem("gate_full"), 1)
        for p in range(2):
            V.tensor_scalar(t1[:, p, :], ps[:, 4 + p, :], vcol(V_BA + p), 0.0, ALU.add, ALU.max)
            V.tensor_scalar(t2[:, p, :], ps[:, 4 + p, :], vcol(V_BA + p), 0.0, ALU.add, ALU.min).then_inc(prep, 1)
            dve.wait_ge(prep, 2 * p + 1)
            V.tensor_tensor(t1[:, p, :], t2[:, p, :], t1[:, p, :], ALU.subtract).then_inc(prep, 1)
        dve.wait_ge(sem("in_mcon"), 32)
        for p in range(2):
            dve.wait_ge(sem("prep_act"), p + 3)
            V.tensor_tensor(t2[:, p, :], t2[:, p, :], t1[:, p, :], ALU.subtract).then_inc(prep, 1)
            dve.wait_ge(prep, 2 * p + 5)
            V.tensor_tensor_scan(scan_b[:, p, :], mcon[:, M_RESET:M_RESET + S], t2[:, p, :], 0.0, ALU.mult, ALU.add).then_inc(prep, 1)
        for p in range(2):
            dve.wait_ge(prep, 2 * p + 6)
            b3 = scan_b[:, p, :].rearrange("q (c t) -> q c t", t=CHUNK)
            V.tensor_tensor(t2[:, p, :].rearrange("q (c t) -> q c t", t=CHUNK),
                            b3[:, :, CHUNK - 1:CHUNK].to_broadcast([P, NCH, CHUNK]), b3, ALU.subtract).then_inc(prep, 1)
        for p in range(2):
            dve.wait_ge(sem("prep_act"), 2 * p + 5)
            wait_full(dve, "qa", p)
            V.scalar_tensor_tensor(q_in[:, p, :], ps[:, pair("qa") + p, :], 0.125, t1[:, p, :], ALU.mult, ALU.mult).then_inc(prep, 1)
        for p in range(2):
            dve.wait_ge(sem("prep_act"), 2 * p + 6)
            wait_full(dve, "ka", p)
            V.tensor_tensor(k_in[:, p, :], ps[:, pair("ka") + p, :], t3[:, p, :], ALU.mult).then_inc(prep, 1)
            dve.wait_ge(sem("prep_act"), p + 9)
            V.tensor_tensor(tmp[:, p, :], ps[:, pair("ka") + p, :], t2[:, p, :], ALU.mult).then_inc(prep, 1)
        mod_block(2)
        dve.wait_ge(prep, 16)
        V.memset(q_raw[:, :, 0:3], 0.0).then_inc(sem("pads_ready"), 1)
        dve.wait_ge(sem("am_full"), 1)
        V.tensor_copy(a_col, ps[:, 6, 0:16]).then_inc(sem("am_copied"), 1)

        def conv(p):
            for b in range(2):
                ch = 2 * p + b
                dve.wait_ge(sem("conv_in"), ch + 1)
                if ch >= 2:
                    dve.wait_ge(sem("qk_ready"), ch - 1)
                else:
                    dve.wait_ge(sem("kd_full"), 2)
                y = tmp[:, b, :]
                tap = lambda k: vcol(V_CW + k * KC + ch)
                link(V.tensor_scalar(y, q_raw[:, ch % CONV_RING, 3:3 + S], tap(3), vcol(V_CB + ch), ALU.mult, ALU.add))
                for k in (2, 1):
                    link(V.scalar_tensor_tensor(y, q_raw[:, ch % CONV_RING, k:k + S], tap(k), y, ALU.mult, ALU.add))
                V.scalar_tensor_tensor(y, q_raw[:, ch % CONV_RING, 0:S], tap(0), y, ALU.mult, ALU.add).then_inc(sem("conv_done"), 1)

        conv(0)
        dve.wait_ge(sem("prep_act"), 10)
        link(V.memset(gla_p[:], 0.0))
        for h in range(4):
            dve.wait_ge(sem("gla_s_full"), h + 1)
            V.copy_predicated(gla_p[:, h, :].rearrange("q (t d) -> q t d", t=TB),
                              mcon[:, M_SAME:M_SAME + P].bitcast(U32).unsqueeze(1).to_broadcast([P, TB, P]),
                              ps[:, GLA_BANK[h], :].rearrange("q (t d) -> q t d", t=TB)).then_inc(sem("gla_p_ready"), 1)
        def states(p):
            for c in range(NCH - 1):
                dve.wait_ge(sem("kv_full"), 2 * p + (1 if c < 4 else 2))
                if c:
                    dve.wait_ge(sem("st_ready"), 7 * p + c)
                for e in range(2):
                    r = slice(64 * e, 64 * e + 64)
                    kv = ps[r, KV_BANK[c], (c // 2 % 2) * 256 + e * P:(c // 2 % 2) * 256 + (e + 1) * P]
                    if c == 0:
                        i = V.tensor_copy(st[r, p, 0, :], kv)
                    else:
                        i = V.scalar_tensor_tensor(st[r, p, c, :], st[r, p, c - 1, :], dec[r, p, c:c + 1], kv, ALU.mult, ALU.add)
                i.then_inc(sem("st_ready"), 1)

        dve.wait_ge(sem("am_full"), 1)
        conv(1)
        states(0)
        conv(2)
        states(1)
        conv(3)
        ada_block(3, False)
        v_blocks("vb")

        for tb in range(TB):
            dve.wait_ge(sem("o_full"), tb + 1)
            if tb == 0:
                dve.wait_ge(sem("ra_ready"), TB)
            for h in range(4):
                i = V.bn_stats(stats[:, 4 * tb + h, :], ps[:, O_BANK[tb], tile_of(h)])
            link(i)
            for h in range(4):
                i = V.bn_aggr(mv[:, 4 * tb + h, :], stats[:, 4 * tb + h, :])
            link(i)
            for h in range(4):
                i = V.scalar_tensor_tensor(og[:, tb, tile_of(h)], ps[:, O_BANK[tb], tile_of(h)], mv[:, 4 * tb + h, 0:1],
                                           og[:, tb, tile_of(h)], ALU.subtract, ALU.mult)
            i.then_inc(sem("o_done"), 1)
        dve.wait_ge(sem("std_gla"), 1)
        link(V.reciprocal(rstd[:], cols[:, 5, :]))
        dve.wait_ge(sem("o_done"), TB)
        V.tensor_tensor(og[:, :, 0:S].rearrange("q t (h d) -> q t h d", h=4), og[:, :, 0:S].rearrange("q t (h d) -> q t h d", h=4),
                        rstd[:].rearrange("q (t h) -> q t h", t=TB).unsqueeze(3).to_broadcast([P, TB, 4, P]),
                        ALU.mult).then_inc(sem("og_ready"), 1)
        dve.wait_ge(sem("o_full"), TB)
        V.memset(cols[:, 2, 0:1], 0.0).then_inc(sem("pv_free"), 1)

        def masked(h):
            dve.wait_ge(sem("ng_full"), h + 1)
            if h == 0:
                dve.wait_ge(sem("qk_ready"), KC)
            V.tensor_tensor(tmp[:, h % 2, :].rearrange("q (t d) -> q t d", t=TB),
                            ps[:, NG_BANK[h % 2], :].rearrange("q (t d) -> q t d", t=TB),
                            mcon[:, M_CAUSAL:M_CAUSAL + P].unsqueeze(1).to_broadcast([P, TB, P]),
                            ALU.add).then_inc(sem("ed_ready"), 1)

        def weigh(h):
            dve.wait_ge(sem("ml_w_ready"), h + 1)
            dve.wait_ge(sem("ml_s_full"), h + 1)
            if h >= 2:
                dve.wait_ge(sem("num_full"), h - 1)
            V.scalar_tensor_tensor(ml_a[:, h % 2, :], psf[:, 0:SC], P ** -0.5, ml_w[:, h % 2, :], ALU.mult, ALU.mult
                                   ).then_inc(sem("ml_a_ready"), 1)

        def ml_stats(h):
            dve.wait_ge(sem("num_ready"), h + 1)
            for tb in range(TB):
                i = V.bn_stats(stats2[:, 4 * h + tb, :], num[:, h, tb, 0:P])
            link(i)
            for tb in range(TB):
                i = V.bn_aggr(mv2[:, 4 * h + tb, :], stats2[:, 4 * h + tb, :])
            link(i)
            if h == 0:
                dve.wait_ge(sem("ob_ready"), TB)
            for tb in range(TB):
                o = og[:, tb, S + h * P:S + (h + 1) * P]
                i = V.scalar_tensor_tensor(o, num[:, h, tb, 0:P], mv2[:, 4 * h + tb, 0:1], o, ALU.subtract, ALU.mult)
            if h == 3:
                link(i)

        masked(0)
        masked(1)
        weigh(0)
        weigh(1)
        for h in range(4):
            if h + 2 < 4:
                dve.wait_ge(sem("ml_w_ready"), h + 1)
                masked(h + 2)
            ml_stats(h)
            if h + 2 < 4:
                weigh(h + 2)
        dve.wait_ge(sem("den_abs"), 1)
        dve.wait_ge(sem("em_ready"), 1)
        link(V.tensor_tensor(cols[:, 3, :].rearrange("q (h t) -> q h t", h=4), cols[:, 2, :].rearrange("q (h t) -> q h t", h=4),
                             em_col.rearrange("q (t h) -> q h t", h=4), ALU.max))
        link(V.reciprocal(cols[:, 3, :], cols[:, 3, :]))
        link(V.tensor_tensor(cols[:, 4, :], mv2[:, :, 1], cols[:, 3, :], ALU.mult))
        V.tensor_tensor(cols[:, 4, :], cols[:, 4, :], cols[:, 3, :], ALU.mult).then_inc(sem("ml_var"), 1)
        dve.wait_ge(sem("ml_std"), 1)
        link(V.reciprocal(rstd[:], cols[:, 4, :]))
        link(V.tensor_tensor(rstd[:], rstd[:], cols[:, 3, :], ALU.mult))
        for h in range(4):
            o = og[:, :, S + h * P:S + (h + 1) * P]
            V.tensor_tensor(o, o, rstd[:, 4 * h:4 * h + 4].unsqueeze(2).to_broadcast([P, TB, P]), ALU.mult
                            ).then_inc(sem("og_ready"), 1)
        for n in range(KC):
            e = H_BASE["cat0"] + n
            dve.wait_ge(sem("cat_full"), n + 1)
            tmp_free(e)
            V.tensor_scalar(tmp[:, e % 2, :], ps[:, 4 + n % 2, :], vcol(V_GN + n), None, ALU.mult).then_inc(sem("h_tmp_ready"), 1)
            if n >= 1:
                lo_of_chunk(e - 1, n - 1)
        lo_of_chunk(H_BASE["cat0"] + KC - 1, KC - 1)

        def norm(i, names, rt, extra={}):
            link(V.tensor_scalar(gate1[:, i, :], mod[:, (2, 5, 8, 11)[i], :], 1.0, None, ALU.add))
            if -1 in extra:
                extra[-1]()
            dve.wait_ge(sem("xa_ready"), KC * (i + 1))

            def part_stats(part):
                lo, hi = (0, 4, 6)[part], (4, 6, 8)[part]
                dve.wait_ge(sem("rt_ready"), KC * i + hi)
                for tb in range(TB):
                    ins = V.bn_stats(stats[:, 3 * tb + part, :], rt[:, tb, lo * P:hi * P])
                return ins

            for n in range(KC):
                wait_full(dve, names[n // 2], n % 2)
                V.scalar_tensor_tensor(xa[:, n, :], ps[:, pair(names[n // 2]) + n % 2, :], gate1[:, i, n:n + 1], xa[:, n, :],
                                       ALU.mult, ALU.add).then_inc(sem("r_ready"), 1)
                if n in extra:
                    extra[n]()
                if n == 3 and i < 3:
                    dve.wait_ge(sem("mod_ready"), (5, 9, 12)[i])
                    derive(i + 1, (3, 6, 9)[i], (4, 7, 10)[i], i)
                if n == 5:
                    part_stats(0)
            part_stats(1)
            link(part_stats(2))
            for tb in range(TB):
                ins = V.bn_aggr(mv[:, tb, :], stats[:, 3 * tb:3 * tb + 3, :].rearrange("p a b -> p (a b)"))
            ins.then_inc(sem("mv_ready"), 1)
            dve.wait_ge(sem("std_ready"), i + 1)
            link(V.reciprocal(rstd[:, 0:TB], cols[:, 5, 0:TB]))
            V.scalar_tensor_tensor(nmr[:], mv[:, 0:TB, 0], -1.0, rstd[:, 0:TB], ALU.mult, ALU.mult).then_inc(sem("nmr_ready"), 1)
            for tb in (0, 2):
                V.tensor_scalar(xh[:, tb, :], rt[:, tb, :], mv[:, tb, 0:1], rstd[:, tb:tb + 1], ALU.subtract, ALU.mult
                                ).then_inc(sem("xh_dve"), 1)
            if i == 3:
                dve.wait_ge(sem("in_rows"), 16)
                for tb in range(TB):
                    dve.wait_ge(sem("xh_act" if tb % 2 else "xh_dve"), 2 * i + tb // 2 + 1)
                    link(V.tensor_tensor(xh[:, tb, :], xh[:, tb, :], rows_gb[:, 0, :], ALU.mult))
                    V.tensor_tensor(xh[:, tb, :], xh[:, tb, :], rows_gb[:, 1, :], ALU.add).then_inc(sem("out_ready"), 1)
                return
            base = H_BASE[f"norm{i}"]
            for n in range(KC):
                name = f"norm{i}_{n // 2}"
                wait_full(dve, name, n % 2)
                chunk_from(base + n, n, ps[:, pair(name) + n % 2, :], i + 1)
                if n >= 1:
                    lo_of_chunk(base + n - 1, n - 1)
            lo_of_chunk(base + KC - 1, KC - 1)

        def ffn(layer):
            s0 = STAGES[f"ffn{layer}"][0]
            f0 = uses[where[f"up{layer}_0"]][1][0][1]
            up = pair(f"up{layer}_0")

            def step(j, first=False):
                for b in range(2):
                    dve.wait_ge(*((sem("bank_full"), 2 * j + f0) if b == 0 else (sem("slot_done"), 4 * j + (s0 + 4))))
                    dve.wait_ge(sem("silu_ready"), 2 * j + (FC * layer + 1 + b))
                    V.tensor_tensor(tmp[:, b, :], tmp[:, b, :], ps[:, up + b, :], ALU.mult).then_inc(sem("prod_ready"), 1)
                for b in range(2):
                    dve.wait_ge(sem("hid_hi_ready"), 2 * j + (FC * layer + 1 + b))
                    at_ = (lambda t: t[:, b, :]) if first else (lambda t: t[:, bass.ds(2 * j + b, 1), :].rearrange("p o t -> p (o t)"))
                    V.tensor_tensor(at_(hid_lo), tmp[:, b, :], at_(hid_hi).bitcast(F32), ALU.subtract).then_inc(sem("hid_ready"), 1)

            step(0, True)
            if layer == 1:
                with dve.Fori(1, FC // 2) as j:
                    step(j)
                return
            with dve.Fori(0, FC // 4) as it:
                dve.wait_ge(sem("ada_cols"), it + 5)
                V.tensor_tensor(mod[:, bass.ds(it + 4, 1), :].rearrange("p o t -> p (o t)"), ps[:, 7, 0:KC],
                                vec[:, bass.ds(KC * it + (V_ADAB + 4 * KC), KC)], ALU.add).then_inc(sem("mod_ready"), 1)
                for u in range(2):
                    for k in range(4 * u, 4 * u + 4):
                        dve.wait_ge(sem(f"ada_landed{k % 2}"), 64 * it + 16 * (12 + k // 2 + 1))
                        if k:
                            dve.wait_ge(sem("ada_step"), 8 * it + (40 + k))
                            V.scalar_tensor_tensor(ada_acc[:], ada_raw[:, k % 2, :], c_act[:, k:k + 1], ada_acc[:], ALU.mult,
                                                   ALU.add).then_inc(sem("ada_step"), 1)
                        else:
                            V.tensor_scalar(ada_acc[:], ada_raw[:, 0, :], c_act[:, 0:1], None, ALU.mult
                                            ).then_inc(sem("ada_step"), 1)
                    step(2 * it + (u + 1))

        norm(0, [f"out0{p}" for p in range(4)], rt_mixer,
             {-1: lambda: ada_block(4, True, range(4)), 1: lambda: ada_block(4, False, range(4, KC)), 3: lambda: mod_block(4)})
        ffn(0)
        norm(1, [f"down0{p}" for p in range(4)], rt_ffn, {-1: lambda: ada_block(10), 1: lambda: ada_block(11)})
        mod_block(11)

        def qk_panel(part):
            name, p = part[:2], int(part[2])
            wait_full(dve, part, 1)
            src = ps[:, pair(part) + 1, :]
            o = {"qc": qc, "kc": kc, "qd": qd, "kd": kd}[name][:, 2 * p + 1, :]
            if name[1] == "d" and p >= 1:
                o, src = o.rearrange("q (t p) -> q t p", t=RES), by_residue(src)
            V.tensor_scalar(o, src, 0.125 if name[0] == "q" else 1.0, None, ALU.mult).then_inc(sem("qk1_dve"), 1)

        qk_panel("qc0")
        qk_panel("qc1")
        dve.wait_ge(sem("f_full"), 1)
        V.tensor_copy(f_rows[:], ps[0:4, 4:7, 0:F_LEN]).then_inc(sem("f_ready"), 1)
        qk_panel("kc0")
        qk_panel("kc1")
        V.memset(vd[:, :, :, 1, :], 1.0)
        v_blocks("vc")

        def diag_tiles(t):
            return (t[:, 0:2 * S].rearrange("q (a x) -> q a x", a=2)[:, :, 0:P], t[:, OFS[3]:OFS[3] + 2 * P].rearrange("q (a x) -> q a x", a=2))

        def twice(ap):
            return ap.unsqueeze(1).to_broadcast([P, 2, P])

        def softplus(h):
            dve.wait_ge(sem("sb_act"), 3 * h + 3)
            if h >= 2:
                dve.wait_ge(sem("tri_full"), h - 1)
            sp_ = sb_sp[h % 2]
            link(V.scalar_tensor_tensor(sp_[:], psf[:, sb_col(h):sb_col(h) + SC], 0.0, sb_a[h % 2][:], ALU.max, ALU.add))
            for t in diag_tiles(sp_):
                i = V.tensor_tensor(t, t, twice(cst[:, C_KEEP:C_KEEP + P]), ALU.mult)
            i.then_inc(sem("sp_ready"), 1)

        def att_mask(h):
            dve.wait_ge(sem("att_exp"), h + 1)
            for t in diag_tiles(sb_a[h % 2]):
                i = V.copy_predicated(t, twice(cst[:, C_DROP:C_DROP + P]).bitcast(U32), zero_col.unsqueeze(1).to_broadcast([P, 2, P]))
            i.then_inc(sem("att_ready"), 1)

        def sb_chunk(n):
            e = H_BASE["cat1"] + n
            dve.wait_ge(sem("av_done"), 2 * n + 2)
            tmp_free(e)
            src = ada_acc[:, 0:S] if n == 0 else ps[:, AV_BANK[n], :]
            V.tensor_copy(tmp[:, e % 2, :], src).then_inc(sem("h_tmp_ready"), 1)
            lo_of_chunk(e, n)

        softplus(0)
        for i, part in enumerate(FILL):
            if part[0] == "v":
                v_blocks(part)
            else:
                qk_panel(part)
            if i % 2 == 0:
                att_mask(i // 2)
            else:
                if i == 3:
                    dve.wait_ge(sem("av_done"), 2)
                    V.tensor_copy(ada_acc[:, 0:S], ps[:, AV_BANK[0], :]).then_inc(sem("staged"), 1)
                softplus(i // 2 + 1)
        dve.wait_ge(sem("staged"), 1)
        sb_chunk(0)
        for h in range(4, 8):
            if h + 1 < 8:
                softplus(h + 1)
            att_mask(h)
            if h % 2 == 0:
                sb_chunk(h // 2 - 1)
        sb_chunk(3)

        dve.wait_ge(sem("av_done"), 8)
        dve.wait_ge(sem("bt_loaded"), 48)
        link(V.memset(lgs[1][:, :, 0, 0:P], NEG))
        for s in range(16):
            h, part = score_step(s)
            dve.wait_ge(sem("l_full"), s + 1)
            ts = part_tiles(part)
            V.tensor_tensor(lg_tiles(h, part), ps[:, score_bank(s), ts[0] * P:S].rearrange("q (t d) -> q t d", d=P),
                            bt_tile(h, part).unsqueeze(1).to_broadcast([P, len(ts), P]), ALU.add).then_inc(sem("l_read"), 1)
            if s % 2 and part % 2:
                dve.wait_ge(sem("l_read"), s + 1)
                for hh in (h - 1, h):
                    i = V.tensor_reduce(mx[:, part // 2, hh:16:TB], lgs[part // 2][:, hh, :, :], mybir.AxisListType.X, ALU.max)
        i.then_inc(sem("dil_mx"), 1)
        dve.wait_ge(sem("mx_turned"), 1)
        V.tensor_copy(m_rows[:], ps[0:4, 4, :]).then_inc(sem("m_half"), 1)
        dve.wait_ge(sem("m_half"), 1)
        V.tensor_tensor(m_rows[:], m_rows[:], ps[0:4, 5, :], ALU.max).then_inc(sem("m_rows_ready"), 1)
        dve.wait_ge(sem("m_turned"), 1)
        V.tensor_scalar(nm, ps[:, 4, 0:32].rearrange("q (a b) -> q a b", a=2), -1.0, None, ALU.mult).then_inc(sem("nm_ready"), 1)

        def dil_out(h):
            e = H_BASE["cat1"] + 4 + h // 2
            r = 64 * (h % 2)
            dve.wait_ge(sem("pv_done"), 4 * h + 4)
            if h % 2 == 0:
                tmp_free(e)
            if h:
                dve.wait_ge(*((sem("dil_out"), h // 2 + 1) if h % 2 else (sem("h_tmp_ready"), H_BASE["cat1"] + 5)))
            link(V.reciprocal(rec[r:r + 64, :], ps[64 - r:P - r, 6 + h % 2, :]))
            V.tensor_tensor(tmp[r:r + 64, e % 2, :], ps[r:r + 64, 6 + h % 2, :], rec[r:r + 64, :], ALU.mult
                            ).then_inc(sem("h_tmp_ready" if h % 2 else "dil_out"), 1)

        for n in range(1, 16, 2):
            dve.wait_ge(sem("turn_full"), n + 1)
            if n >= 4:
                dve.wait_ge(sem("pv_done"), n - 3)
            V.tensor_copy(pt[:, n % 4, :], ps[:, n % 4, :]).then_inc(sem("turn_dve"), 1)
            if n == 13:
                lo_of_chunk(H_BASE["cat1"] + 4, 4)
            if n % 4 == 1 and n >= 5:
                dil_out(n // 4 - 1)
        dil_out(3)
        lo_of_chunk(H_BASE["cat1"] + 5, 5)
        norm(2, [f"out1{p}" for p in range(4)], rt_mixer)
        ffn(1)
        norm(3, [f"down1{p}" for p in range(4)], rt_ffn)

    ctx.close()


def weight_stream(w):
    s = np.zeros((N_SLOTS, P, SLOT), np.float32)

    def tiles(a, k, n):
        return a.reshape(k, P, n).transpose(1, 0, 2).reshape(P, k * n)

    def panel(name, a, nk):
        first = STAGES[name][0]
        for i, (k0, n) in enumerate(panel_slots(nk)):
            s[first + i, :, :n * 256] = tiles(a[k0 * P:(k0 + n) * P], n, 256)

    def group(name, a, kk, width):
        first, count = STAGES[name]
        for i in range(count):
            s[first + i] = tiles(a[i * kk * P:(i + 1) * kk * P], kk, width)

    ab, cd = w["ab_w_in"][0], w["cd_w_in"][0]
    narrow = np.zeros((D, P), np.float32)
    narrow[:, 0:16] = ab[:, 1536:1552]
    narrow[:, 32:36] = ab[:, 3088:3092]
    narrow[:, 64:68] = ab[:, 3092:3096]
    s[0] = tiles(narrow, KC, P)
    panel("qa", ab[:, 0:256], KC)
    panel("ka", ab[:, 256:512], KC)
    group("va", ab[:, 512:1024], 2, S)
    for p in range(4):
        panel(f"qkb{p}", ab[:, 1552 + 256 * p:1808 + 256 * p], KC)
    group("vb", ab[:, 2576:3088], 2, S)
    group("ra", ab[:, 1024:1536], 2, S)
    group("ob", ab[:, 3096:3608], 2, S)
    for layer, wo, nk in ((0, w["ab_w_out"][0], KC), (1, w["cd_w_out"][0], 6)):
        for p in range(4):
            panel(f"out{layer}{p}", wo[:, 256 * p:256 * (p + 1)], nk)
            panel(f"down{layer}{p}", w["ffn_w2"][layer][:, 256 * p:256 * (p + 1)], FC)
        for j in range(FC // 2):
            first = STAGES[f"ffn{layer}"][0] + 4 * j
            for i, a in enumerate((w["ffn_w1"][layer], w["ffn_w3"][layer])):
                for half in range(2):
                    s[first + 2 * i + half] = tiles(a[512 * half:512 * (half + 1), 256 * j:256 * (j + 1)], 4, 256)
    col = 0
    for name, panels in (("qc", 2), ("kc", 2)):
        for p in range(panels):
            panel(f"{name}{p}", cd[:, col:col + 256], KC)
            col += 256
    group("vc", cd[:, col:col + 512], 2, S)
    col += 512
    for name, panels in (("qd", 3), ("kd", 3)):
        for p in range(panels):
            panel(f"{name}{p}", cd[:, col:col + 256], KC)
            col += 256
    group("vd0", cd[:, col + 256:col + 768], 2, S)
    group("vd1", cd[:, col:col + 256], 4, 256)
    return s


def kernel(**inputs):
    import concourse.bacc as bacc
    from concourse.bass_utils import run_bass_kernel_spmd

    w = {k: np.asarray(v) for k, v in inputs.items()}
    chunks = lambda a: a.reshape(-1, P).T
    vecs = np.zeros((P, V_N), np.float32)
    vecs[:, V_C:V_C + KC] = chunks(w["c"])
    vecs[:, V_ADAB:V_ADAB + 96] = chunks(w["ada_b"])
    vecs[:, V_LNG:V_LNG + 32] = chunks(w["ln_g"])
    vecs[:, V_LNB:V_LNB + 32] = chunks(w["ln_b"])
    vecs[:, V_BA:V_BA + 2] = chunks(w["gla_ba"])
    vecs[:, V_GN:V_GN + 4] = chunks(w["gla_norm_g"])
    vecs[:, V_GN + 4:V_GN + 8] = chunks(w["ml_norm_g"])
    vecs[:, V_CW:V_CW + 32] = chunks(w["ml_conv_w"])
    vecs[:, V_CB:V_CB + KC] = chunks(w["ml_conv_b"])
    vecs[32:36, V_BI] = w["ml_b_i"][0]
    vecs[64:68, V_BF] = w["ml_b_f"][0]
    const, const0 = constants()
    rel = np.ones((N_BUCKETS + 1, 12), np.float32)
    rel[0:N_BUCKETS] = w["rel_bias"]
    ada = w["ada_w"].reshape(2, KC, P, 6, D).transpose(0, 3, 1, 2, 4).reshape(12 * KC, P, D)
    arrays = {
        "wstream": weight_stream(w),
        "astream": np.ascontiguousarray(ada),
        "xT": np.ascontiguousarray(w["x"][0].T),
        "vecs": vecs,
        "const": const,
        "const0": const0,
        "wa_up": np.ascontiguousarray(w["gla_wa_up"][0]),
        "dsel": distance_select(),
        "rel": rel,
        "ln_rows": np.ascontiguousarray(np.broadcast_to(np.stack([w["ln_g"][1, 1], w["ln_b"][1, 1]]), (P, 2, D))),
    }
    nc = bacc.Bacc("TRN2", target_bir_lowering=False, num_devices=1)
    args = {n: nc.dram_tensor(n, a.shape, F32, kind="ExternalInput").ap() for n, a in arrays.items()}
    out = nc.dram_tensor("out", (S, D), F32, kind="ExternalOutput").ap()
    build_program(nc, **args, out=out)
    r = run_bass_kernel_spmd(nc, [arrays], core_ids=[0])
    return r.results[0]["out"].reshape(1, S, D)
```
